# Optimizing a Trainium2 kernel written in Bass

```python
import math
import jax, jax.numpy as jnp
from jax import lax
import numpy as np

D_MODEL = 1024
BATCH = 1
SEQ = 1024
DEPTH = 1

D_MIX = D_MODEL
HEAD_DIM = 64
RWKV_WIDTH = D_MIX // 2
SB_WIDTH = D_MIX - RWKV_WIDTH
RWKV_HEADS = RWKV_WIDTH // HEAD_DIM
SB_HEADS = SB_WIDTH // HEAD_DIM
DECAY_LORA = 64
ICLR_LORA = 64
SHIFT_COLS = 3 * RWKV_WIDTH + DECAY_LORA + ICLR_LORA
RWKV_COLS = SHIFT_COLS + RWKV_WIDTH
SB_COLS = 4 * SB_WIDTH
IN_COLS = RWKV_COLS + SB_COLS
Q_BLOCK = 128
NORM_EPS = 1e-6
GN_EPS = 64e-5


def rmsnorm(x, g):
    xf = x.astype(jnp.float32)
    y = xf * lax.rsqrt(jnp.mean(xf * xf, axis=-1, keepdims=True) + NORM_EPS)
    return (y * g.astype(jnp.float32)).astype(x.dtype)

def rwkv7_group(p, mu, w0, w2, a0, a2, k_k, k_a, r_k, ln_w, ln_b):
    B, S, _ = p.shape
    H, N = RWKV_HEADS, HEAD_DIM
    ps, g = p[..., :SHIFT_COLS], p[..., SHIFT_COLS:]
    prev = jnp.pad(ps, ((0, 0), (1, 0), (0, 0)))[:, :-1]
    ps = ps + (prev - ps) * mu
    r, k, v, zw, za = jnp.split(
        ps, [RWKV_WIDTH, 2 * RWKV_WIDTH, 3 * RWKV_WIDTH, 3 * RWKV_WIDTH + DECAY_LORA], axis=-1)
    w_log = -jax.nn.softplus(-(w0 + jnp.tanh(zw) @ w2)) - 0.5
    decay = jnp.exp(-jnp.exp(w_log.astype(jnp.float32)))
    a = jax.nn.sigmoid(a0 + za @ a2)
    hd = lambda t: t.reshape(B, S, H, N)
    r, k, v, decay, a = hd(r), hd(k), hd(v), hd(decay), hd(a)
    kk = hd(ps[..., RWKV_WIDTH:2 * RWKV_WIDTH] * k_k)
    kkf = kk.astype(jnp.float32)
    kk = kkf * lax.rsqrt(jnp.maximum(jnp.sum(kkf * kkf, axis=-1, keepdims=True), 1e-24))
    k = k * (1.0 + (a - 1.0) * k_a.reshape(H, N))

    def step(state, inp):
        r_t, w_t, k_t, v_t, kk_t, b_t = inp
        sa = jnp.einsum('bhij,bhj->bhi', state, -kk_t)
        state = (state * w_t[:, :, None, :]
                 + sa[..., None] * b_t[:, :, None, :]
                 + v_t[..., None] * k_t[:, :, None, :])
        y_t = jnp.einsum('bhij,bhj->bhi', state, r_t)
        return state, y_t

    tm = lambda t: jnp.moveaxis(t.astype(jnp.float32), 1, 0)
    state0 = jnp.zeros((B, H, N, N), jnp.float32)
    _, y = lax.scan(step, state0, (tm(r), tm(decay), tm(k), tm(v), tm(kk), tm(kk * a)))
    y = jnp.moveaxis(y, 0, 1)
    mean = jnp.mean(y, axis=-1, keepdims=True)
    var = jnp.mean(jnp.square(y - mean), axis=-1, keepdims=True)
    y = (y - mean) * lax.rsqrt(var + GN_EPS)
    y = y * ln_w.reshape(H, N) + ln_b.reshape(H, N)
    rf, kf, vf = r.astype(jnp.float32), k.astype(jnp.float32), v.astype(jnp.float32)
    y = y + jnp.sum(rf * kf * r_k, axis=-1, keepdims=True) * vf
    y = y.reshape(B, S, RWKV_WIDTH).astype(p.dtype)
    return y * jax.nn.silu(g)

def stick_breaking_group(p, sb_g):
    B, S, _ = p.shape
    H, N = SB_HEADS, HEAD_DIM
    n_blocks = S // Q_BLOCK
    q, k, v, g = jnp.split(p, 4, axis=-1)
    hd = lambda t: t.reshape(B, S, H, N).transpose(0, 2, 1, 3)
    q, k, v = hd(q), hd(k), hd(v)
    scale = 1.0 / math.sqrt(N)
    k_pos = jnp.arange(S)
    q_blocks = q.reshape(B, H, n_blocks, Q_BLOCK, N).transpose(2, 0, 1, 3, 4)

    def block(args):
        q_blk, idx = args
        q_pos = idx * Q_BLOCK + jnp.arange(Q_BLOCK)
        z = jnp.einsum('bhqd,bhkd->bhqk', q_blk, k).astype(jnp.float32) * scale
        mask = k_pos[None, :] < q_pos[:, None]
        log_1m = jnp.where(mask, jax.nn.log_sigmoid(-z), 0.0)
        after = lax.cumsum(log_1m, axis=3, reverse=True) - log_1m
        attn = jnp.where(mask, jnp.exp(jax.nn.log_sigmoid(z) + after), 0.0)
        return jnp.einsum('bhqk,bhkd->bhqd', attn.astype(v.dtype), v)

    o = lax.map(block, (q_blocks, jnp.arange(n_blocks)))
    o = o.transpose(1, 3, 0, 2, 4).reshape(B, S, H, N)
    o = rmsnorm(o, sb_g.reshape(H, N)).reshape(B, S, SB_WIDTH)
    return o * jax.nn.silu(g)

def first_inputs(seed: int = 0) -> dict:
    key = jax.random.key(seed)
    ks = jax.random.split(key, 20)
    nrm = lambda k, shape, s: s * jax.random.normal(k, shape, jnp.float32)
    return {
        "x": nrm(ks[0], (BATCH, SEQ, D_MODEL), 1.0),
        "c": nrm(ks[1], (BATCH, D_MODEL), 1.0),
        "norm_g": 1.0 + nrm(ks[2], (DEPTH, D_MODEL), 0.05),
        "ada_w": nrm(ks[3], (DEPTH, D_MODEL, 3 * D_MODEL), 0.5 * D_MODEL ** -0.5),
        "ada_b": nrm(ks[4], (DEPTH, 3 * D_MODEL), 0.02),
        "w_in": nrm(ks[5], (DEPTH, D_MODEL, IN_COLS), D_MODEL ** -0.5),
        "w_out": nrm(ks[6], (DEPTH, D_MIX, D_MODEL), D_MIX ** -0.5),
        "tshift_mu": jax.random.uniform(ks[7], (DEPTH, SHIFT_COLS), jnp.float32),
        "decay_w0": jax.random.uniform(ks[8], (DEPTH, RWKV_WIDTH), jnp.float32, minval=-4.0, maxval=1.0),
        "decay_w2": nrm(ks[9], (DEPTH, DECAY_LORA, RWKV_WIDTH), 0.5 * DECAY_LORA ** -0.5),
        "iclr_a0": nrm(ks[10], (DEPTH, RWKV_WIDTH), 0.5),
        "iclr_a2": nrm(ks[11], (DEPTH, ICLR_LORA, RWKV_WIDTH), 0.5 * ICLR_LORA ** -0.5),
        "k_k": 0.85 + nrm(ks[12], (DEPTH, RWKV_WIDTH), 0.05),
        "k_a": 1.0 + nrm(ks[13], (DEPTH, RWKV_WIDTH), 0.05),
        "r_k": nrm(ks[14], (DEPTH, RWKV_HEADS, HEAD_DIM), 0.1),
        "rwkv_ln_w": 1.0 + nrm(ks[15], (DEPTH, RWKV_WIDTH), 0.05),
        "rwkv_ln_b": nrm(ks[16], (DEPTH, RWKV_WIDTH), 0.02),
        "sb_norm_g": 1.0 + nrm(ks[17], (DEPTH, SB_WIDTH), 0.05),
        "final_g": 1.0 + nrm(ks[18], (D_MODEL,), 0.05),
    }

def first_block(x, c, norm_g, ada_w, ada_b, w_in, w_out, tshift_mu, decay_w0, decay_w2,
              iclr_a0, iclr_a2, k_k, k_a, r_k, rwkv_ln_w, rwkv_ln_b, sb_norm_g, final_g):
    c_act = jax.nn.silu(c)
    for l in range(DEPTH):
        mod = c_act @ ada_w[l] + ada_b[l]
        shift, scale, gate = jnp.split(mod, 3, axis=-1)
        h = rmsnorm(x, norm_g[l]) * (1.0 + scale[:, None, :]) + shift[:, None, :]
        p = h @ w_in[l]
        y_rwkv = rwkv7_group(p[..., :RWKV_COLS], tshift_mu[l], decay_w0[l], decay_w2[l],
                             iclr_a0[l], iclr_a2[l], k_k[l], k_a[l], r_k[l],
                             rwkv_ln_w[l], rwkv_ln_b[l])
        y_sb = stick_breaking_group(p[..., RWKV_COLS:], sb_norm_g[l])
        y = jnp.concatenate([y_rwkv, y_sb], axis=-1) @ w_out[l]
        x = x + gate[:, None, :] * y
    return rmsnorm(x, final_g)


GRID_W = 64
CTX_LEN = 256
N_MIXERS = 2
N_A_LAYERS = (DEPTH + N_MIXERS - 1) // N_MIXERS
N_B_LAYERS = DEPTH // N_MIXERS
EPS = 1e-6
HG_EXPAND = 128
HG_HEADS = D_MODEL // HG_EXPAND
HG_DK = HG_EXPAND
HG_DV = D_MODEL // HG_HEADS
HG_F = HG_HEADS * HG_DK
CHUNK = 64
D_RNN = D_MODEL
LRU_BLOCKS = 4
LRU_BW = D_RNN // LRU_BLOCKS
LRU_CONV_W = 4
LRU_C = 8.0
D_FF = 2816
FFN_CONV_W = 3


def rmsnorm_2(x, g):
    xf = x.astype(jnp.float32)
    y = xf * lax.rsqrt(jnp.mean(xf * xf, axis=-1, keepdims=True) + EPS)
    return (y * g).astype(x.dtype)

def modulate(h, shift, scale):
    return h * (1.0 + scale) + shift

def dwconv(x, w, b):
    K = w.shape[0]
    right = (K - 1) // 2
    left = K - 1 - right
    T = x.shape[1]
    xp = jnp.pad(x, ((0, 0), (left, right), (0, 0)))
    return sum(w[k] * xp[:, k:k + T] for k in range(K)) + b

def _flip(t, d, axis):
    return t if d == 0 else jnp.flip(t, axis=axis)

def hgrn2_chunk_scan(q, k, v, logf, s0):
    Bn, H, T, _ = q.shape
    n = T // CHUNK
    rs = lambda t: t.reshape(Bn, H, n, CHUNK, t.shape[-1])
    q, k, v, logf = rs(q), rs(k), rs(v), rs(logf)
    b = jnp.cumsum(logf, axis=3)
    b_ref = b[:, :, :, CHUNK // 2:CHUNK // 2 + 1]
    b_last = b[:, :, :, -1:]
    qe = q * jnp.exp(b - b_ref)
    ke = k * jnp.exp(b_ref - b)
    scores = jnp.einsum('bhnik,bhnjk->bhnij', qe, ke)
    mask = jnp.tril(jnp.ones((CHUNK, CHUNK), dtype=bool))
    scores = jnp.where(mask, scores, 0.0)
    o_intra = jnp.einsum('bhnij,bhnjv->bhniv', scores, v)
    kv = jnp.einsum('bhnjk,bhnjv->bhnkv', k * jnp.exp(b_last - b), v)
    decay = jnp.exp(b_last[:, :, :, 0])

    def step(s, inp):
        dcy, u = inp
        return dcy[..., None] * s + u, s

    s_final, s_start = lax.scan(step, s0, (jnp.moveaxis(decay, 2, 0), jnp.moveaxis(kv, 2, 0)))
    s_start = jnp.moveaxis(s_start, 0, 2)
    o_inter = jnp.einsum('bhnik,bhnkv->bhniv', q * jnp.exp(b), s_start)
    o = (o_intra + o_inter).reshape(Bn, H, T, v.shape[-1])
    return o, s_final

def hgrn2_mixer(h_ctx, h_lat, w_in, lb, g_gain, w_out, need_ctx):
    def prep(h):
        Bn, T, _ = h.shape
        heads = lambda t: t.reshape(Bn, T, HG_HEADS, -1).transpose(0, 2, 1, 3)
        q, zf_fwd, zf_bwd, v, g = jnp.split(h @ w_in, 5, axis=-1)
        q = heads(jax.nn.silu(q))
        v = heads(v)
        logf, k = [], []
        for d, zf in enumerate((zf_fwd, zf_bwd)):
            f = lb[d] + (1.0 - lb[d]) * jax.nn.sigmoid(zf.astype(jnp.float32))
            logf.append(heads(jnp.log(f)))
            k.append(heads(1.0 - f))
        return q, k, v, logf, g

    qc, kc, vc, lfc, gc = prep(h_ctx)
    ql, kl, vl, lfl, gl = prep(h_lat)
    s0 = jnp.zeros((h_lat.shape[0], HG_HEADS, HG_DK, HG_DV), jnp.float32)
    o_c, o_l = 0.0, 0.0
    for d in range(2):
        oc_d, s_ctx = hgrn2_chunk_scan(_flip(qc, d, 2), _flip(kc[d], d, 2), _flip(vc, d, 2),
                                       _flip(lfc[d], d, 2), s0)
        ol_d, _ = hgrn2_chunk_scan(_flip(ql, d, 2), _flip(kl[d], d, 2), _flip(vl, d, 2),
                                   _flip(lfl[d], d, 2), s_ctx)
        o_c = o_c + _flip(oc_d, d, 2)
        o_l = o_l + _flip(ol_d, d, 2)

    def readout(o, g):
        Bn, H, T, DV = o.shape
        o = rmsnorm_2(o, g_gain).transpose(0, 2, 1, 3).reshape(Bn, T, H * DV)
        return (o * jax.nn.silu(g)) @ w_out

    y_c = readout(o_c, gc) if need_ctx else None
    return y_c, readout(o_l, gl)

def lru_scan(log_a, u, h0):
    a = jnp.exp(log_a)
    u = u.at[:, 0].add(a[:, 0] * h0)

    def combine(l, r):
        al, ul = l
        ar, ur = r
        return al * ar, ar * ul + ur

    _, h = lax.associative_scan(combine, (a, u), axis=1)
    return h

def rglru_mixer(h_ctx, h_lat, w_in, conv_w, conv_b, wa, ba, wx, bx, lam, w_out, need_ctx):
    Bn, T, _ = h_lat.shape
    rows = T // GRID_W
    to_cm = lambda t: t.reshape(Bn, rows, GRID_W, -1).transpose(0, 2, 1, 3).reshape(Bn, T, -1)
    from_cm = lambda t: t.reshape(Bn, GRID_W, rows, -1).transpose(0, 2, 1, 3).reshape(Bn, T, -1)

    def branch(h):
        gate, xr = jnp.split(h @ w_in, 2, axis=-1)
        return gate, dwconv(xr, conv_w, conv_b)

    def gates(xr, d):
        xb = xr.reshape(*xr.shape[:-1], LRU_BLOCKS, LRU_BW)
        r = jax.nn.sigmoid(jnp.einsum('btnk,nkj->btnj', xb, wa[d]).reshape(xr.shape) + ba[d])
        i = jax.nn.sigmoid(jnp.einsum('btnk,nkj->btnj', xb, wx[d]).reshape(xr.shape) + bx[d])
        log_a = -LRU_C * r.astype(jnp.float32) * jax.nn.softplus(-lam[d].astype(jnp.float32))
        mult = jnp.sqrt(-jnp.expm1(2.0 * log_a))
        return log_a, mult * (i * xr)

    gate_c, xc = branch(h_ctx)
    gate_l, xl = branch(to_cm(h_lat))
    h0 = jnp.zeros((Bn, D_RNN), jnp.float32)
    y_c, y_l = 0.0, 0.0
    for d in range(2):
        la_c, u_c = gates(_flip(xc, d, 1), d)
        hc = lru_scan(la_c, u_c, h0)
        la_l, u_l = gates(_flip(xl, d, 1), d)
        hl = lru_scan(la_l, u_l, hc[:, -1])
        y_c = y_c + _flip(hc, d, 1)
        y_l = y_l + _flip(hl, d, 1)
    out_l = from_cm(y_l * jax.nn.gelu(gate_l)) @ w_out
    out_c = (y_c * jax.nn.gelu(gate_c)) @ w_out if need_ctx else None
    return out_c, out_l

def conv_ffn(h, w_up, conv_w, conv_b, w_down):
    u = dwconv(h @ w_up, conv_w, conv_b)
    gate, val = jnp.split(u, 2, axis=-1)
    return (jax.nn.silu(gate) * val) @ w_down

def second_inputs(seed: int = 0) -> dict:
    key = jax.random.key(seed)
    ks = iter(jax.random.split(key, 32))
    nrm = lambda shape, s: jax.random.normal(next(ks), shape, jnp.float32) * s
    D = D_MODEL
    a0 = jax.random.uniform(next(ks), (N_B_LAYERS, 2, D_RNN), jnp.float32, 0.9, 0.999)
    sig = a0 ** (1.0 / LRU_C)
    lam = jnp.log(sig) - jnp.log1p(-sig)
    return {
        "x": nrm((BATCH, SEQ, D), 1.0),
        "c": nrm((BATCH, D), 1.0),
        "ctx": nrm((BATCH, CTX_LEN, D), 1.0),
        "c_ctx": nrm((D,), 1.0),
        "w_ada": nrm((DEPTH, D, 6 * D), D ** -0.5),
        "b_ada": nrm((DEPTH, 6 * D), 0.02),
        "norm_g": 1.0 + nrm((DEPTH, 2, D), 0.02),
        "hg_w_in": nrm((N_A_LAYERS, D, 5 * D), D ** -0.5),
        "hg_lb_logits": nrm((N_A_LAYERS + 1, 2, HG_F), 0.1),
        "hg_gnorm": 1.0 + nrm((N_A_LAYERS, HG_DV), 0.02),
        "hg_w_out": nrm((N_A_LAYERS, D, D), D ** -0.5),
        "lru_w_in": nrm((N_B_LAYERS, D, 2 * D_RNN), D ** -0.5),
        "lru_conv_w": nrm((N_B_LAYERS, LRU_CONV_W, D_RNN), LRU_CONV_W ** -0.5),
        "lru_conv_b": nrm((N_B_LAYERS, D_RNN), 0.02),
        "lru_wa": nrm((N_B_LAYERS, 2, LRU_BLOCKS, LRU_BW, LRU_BW), LRU_BW ** -0.5),
        "lru_ba": nrm((N_B_LAYERS, 2, D_RNN), 0.02),
        "lru_wx": nrm((N_B_LAYERS, 2, LRU_BLOCKS, LRU_BW, LRU_BW), LRU_BW ** -0.5),
        "lru_bx": nrm((N_B_LAYERS, 2, D_RNN), 0.02),
        "lru_lambda": lam,
        "lru_w_out": nrm((N_B_LAYERS, D_RNN, D), D_RNN ** -0.5),
        "ffn_w_up": nrm((DEPTH, D, 2 * D_FF), D ** -0.5),
        "ffn_conv_w": nrm((DEPTH, FFN_CONV_W, 2 * D_FF), FFN_CONV_W ** -0.5),
        "ffn_conv_b": nrm((DEPTH, 2 * D_FF), 0.02),
        "ffn_w_down": nrm((DEPTH, D_FF, D), D_FF ** -0.5),
        "final_g": 1.0 + nrm((D,), 0.02),
    }

def second_block(x, c, ctx, c_ctx, w_ada, b_ada, norm_g, hg_w_in, hg_lb_logits, hg_gnorm, hg_w_out,
              lru_w_in, lru_conv_w, lru_conv_b, lru_wa, lru_ba, lru_wx, lru_bx, lru_lambda, lru_w_out,
              ffn_w_up, ffn_conv_w, ffn_conv_b, ffn_w_down, final_g):
    lower_bounds = jnp.cumsum(jax.nn.softmax(hg_lb_logits.astype(jnp.float32), axis=0), axis=0)
    lat, cx = x, ctx
    sc_lat, sc_ctx = jax.nn.silu(c), jax.nn.silu(c_ctx)
    for l in range(DEPTH):
        last = l == DEPTH - 1
        m_l = (sc_lat @ w_ada[l] + b_ada[l])[:, None, :]
        m_c = sc_ctx @ w_ada[l] + b_ada[l]
        sh1, sc1, g1, sh2, sc2, g2 = jnp.split(m_l, 6, axis=-1)
        csh1, csc1, cg1, csh2, csc2, cg2 = jnp.split(m_c, 6, axis=-1)
        hl = modulate(rmsnorm_2(lat, norm_g[l, 0]), sh1, sc1)
        hc = modulate(rmsnorm_2(cx, norm_g[l, 0]), csh1, csc1)
        j = l // N_MIXERS
        if l % N_MIXERS == 0:
            yc, yl = hgrn2_mixer(hc, hl, hg_w_in[j], lower_bounds[j], hg_gnorm[j], hg_w_out[j],
                                 not last)
        else:
            yc, yl = rglru_mixer(hc, hl, lru_w_in[j], lru_conv_w[j], lru_conv_b[j], lru_wa[j],
                                 lru_ba[j], lru_wx[j], lru_bx[j], lru_lambda[j], lru_w_out[j],
                                 not last)
        lat = lat + g1 * yl
        hl = modulate(rmsnorm_2(lat, norm_g[l, 1]), sh2, sc2)
        lat = lat + g2 * conv_ffn(hl, ffn_w_up[l], ffn_conv_w[l], ffn_conv_b[l], ffn_w_down[l])
        if not last:
            cx = cx + cg1 * yc
            hc = modulate(rmsnorm_2(cx, norm_g[l, 1]), csh2, csc2)
            cx = cx + cg2 * conv_ffn(hc, ffn_w_up[l], ffn_conv_w[l], ffn_conv_b[l], ffn_w_down[l])
    return rmsnorm_2(lat, final_g)


def setup_inputs(seed=0):
    out = dict(first_inputs(seed))
    for name, value in second_inputs(seed + 1).items():
        if name != "x":
            out[name + "_2"] = value
    return out


def reference(
    x, c, norm_g, ada_w, ada_b, w_in, w_out, tshift_mu, decay_w0, decay_w2, iclr_a0, iclr_a2,
    k_k, k_a, r_k, rwkv_ln_w, rwkv_ln_b, sb_norm_g, final_g, c_2, ctx_2, c_ctx_2, w_ada_2,
    b_ada_2, norm_g_2, hg_w_in_2, hg_lb_logits_2, hg_gnorm_2, hg_w_out_2, lru_w_in_2,
    lru_conv_w_2, lru_conv_b_2, lru_wa_2, lru_ba_2, lru_wx_2, lru_bx_2, lru_lambda_2,
    lru_w_out_2, ffn_w_up_2, ffn_conv_w_2, ffn_conv_b_2, ffn_w_down_2, final_g_2,
):
    x = first_block(
        x, c, norm_g, ada_w, ada_b, w_in, w_out, tshift_mu, decay_w0, decay_w2, iclr_a0,
        iclr_a2, k_k, k_a, r_k, rwkv_ln_w, rwkv_ln_b, sb_norm_g, final_g,
    )
    return second_block(
        x, c_2, ctx_2, c_ctx_2, w_ada_2, b_ada_2, norm_g_2, hg_w_in_2, hg_lb_logits_2,
        hg_gnorm_2, hg_w_out_2, lru_w_in_2, lru_conv_w_2, lru_conv_b_2, lru_wa_2, lru_ba_2,
        lru_wx_2, lru_bx_2, lru_lambda_2, lru_w_out_2, ffn_w_up_2, ffn_conv_w_2, ffn_conv_b_2,
        ffn_w_down_2, final_g_2,
    )


_drawn_inputs = setup_inputs


def setup_inputs(seed=0):
    import zlib

    import numpy as np

    out = dict(_drawn_inputs(seed))
    spreads = {}
    factors = {'norm_g': 2.755,
     'ada_b': 2.903,
     'decay_w2': 4.706,
     'k_k': 51.157,
     'k_a': 5.408,
     'rwkv_ln_w': 7.183,
     'rwkv_ln_b': 28.848,
     'sb_norm_g': 7.45,
     'ctx_2': 6.814,
     'c_ctx_2': 4.966,
     'norm_g_2': 3.677,
     'hg_lb_logits_2': 8.0,
     'hg_gnorm_2': 6.519,
     'ffn_conv_b_2': 17.132,
     'final_g_2': 8.198}
    for name, (base, spread) in spreads.items():
        noise = np.random.default_rng([zlib.crc32(name.encode()), seed]).standard_normal(out[name].shape)
        drawn = base * np.exp(spread * noise) if base else spread * noise
        out[name] = __import__('jax').numpy.asarray(drawn.astype(out[name].dtype))
    for name, factor in factors.items():
        out[name] = (out[name] * factor).astype(out[name].dtype)
    return out
```

```python
import math
from contextlib import ExitStack

import numpy as np

import concourse.bass as bass
from concourse import mybir
from concourse.alu_op_type import AluOpType as ALU

F32 = mybir.dt.float32
I32 = mybir.dt.int32
BF16 = mybir.dt.bfloat16
ACT = mybir.ActivationFunctionType

P = 128
SEQ = 1024
D = 1024
KT = D // P
TT = SEQ // P
BANK = 512
NB = SEQ // BANK
CTX = 256
HD = 64
HG_CHUNK = 32
PER_TILE = P // HG_CHUNK
SCORE_SCALE = 2.0 ** -30
DFF = 2816
FT = DFF // P
NORM_EPS = 1e-6
GN_EPS = 64e-5

IN_R, IN_K, IN_V, IN_Z, IN_G, SB_Q, SB_K, SB_V, SB_G = 0, 4, 8, 12, 13, 17, 21, 25, 29
HG_Q, HG_F, HG_I, HG_G = 0, 8, 24, 32

COLUMNS = [
    ("c", 8), ("norm_g", 8), ("ada_b", 24), ("mu", 13), ("w0", 4), ("a0", 4), ("k_k", 4), ("k_a", 4),
    ("r_k", 4), ("ln_w", 4), ("ln_b", 4), ("sb_g", 4), ("final_g", 8), ("c_2", 8), ("c_ctx_2", 8),
    ("b_ada_2", 48), ("norm_g_2", 16), ("lb_logits", 32), ("gnorm", 1), ("conv_w", 3 * 2 * FT),
    ("conv_b", 2 * FT), ("final_g_2", 8),
]
COL_AT = {}
_n = 0
for _name, _w in COLUMNS:
    COL_AT[_name] = _n
    _n += _w
NCOLS = _n

FCONST = ["ident", "ones", "pair_ones", "at_or_after", "before", "key_before_query", "hg_fwd", "hg_bwd"]
ICONST = ["lt", "le"] + [f"low{n}" for n in (1, 2, 4, 8, 16, 32)] + \
         [f"up{n}" for n in (1, 2, 4, 8, 16, 32, 64)]


def constants():
    i, j = np.meshgrid(np.arange(P), np.arange(P), indexing="ij")
    f = {
        "ident": i == j, "ones": i >= 0, "pair_ones": i // HD == j // HD,
        "at_or_after": i >= j, "before": i < j,
        "key_before_query": i < j,
        "hg_fwd": (i // HG_CHUNK == j // HG_CHUNK) & (i <= j),
        "hg_bwd": (i // HG_CHUNK == j // HG_CHUNK) & (i >= j),
    }
    m = {"lt": i < j, "le": i <= j}
    for n in (1, 2, 4, 8, 16, 32, 64):
        low = (i // (2 * n) == j // (2 * n)) & (i % (2 * n) >= n) & (j % (2 * n) < n)
        m[f"low{n}"], m[f"up{n}"] = low, low.T
    return (np.concatenate([f[n].astype(np.float32) for n in FCONST], 1),
            np.concatenate([m[n].astype(np.int32) for n in ICONST], 1))


class Queue:

    def __init__(self, sem):
        self.sem, self.count, self.program, self.waited = sem, 0, [], {}

    def wait(self, marks):
        for sem, value in marks:
            if self.waited.get(sem.name, 0) < value:
                self.waited[sem.name] = value
                self.program.append(lambda e, sem=sem, value=value: e.wait_ge(sem, value))

    def add(self, make, wait=(), mark=True):
        self.wait(wait)
        if not mark:
            self.program.append(make)
            return None
        self.count += 1
        self.program.append(lambda e: make(e).then_inc(self.sem, 1))
        return (self.sem, self.count)

    def last(self):
        return [(self.sem, self.count)] if self.count else []

    def act(self, out, in_, func, wait=(), **kw):
        return self.add(lambda e: e.activation(out, in_, func, **kw), wait)

    def tt(self, out, a, b, op, wait=()):
        return self.add(lambda e: e.tensor_tensor(out, a, b, op), wait)

    def ts(self, out, a, s1, s2, op0, op1=None, wait=()):
        if op1 is None:
            return self.add(lambda e: e.tensor_scalar(out, a, s1, None, op0), wait)
        return self.add(lambda e: e.tensor_scalar(out, a, s1, s2, op0, op1), wait)

    def stt(self, out, a, s, b, op0, op1, wait=()):
        return self.add(lambda e: e.scalar_tensor_tensor(out=out, in0=a, scalar=s, in1=b, op0=op0, op1=op1), wait)

    def copy(self, out, in_, wait=()):
        return self.add(lambda e: e.tensor_copy(out, in_), wait)

    def fill(self, out, value, wait=()):
        return self.add(lambda e: e.memset(out, value), wait)

    def select(self, out, mask, data, wait=()):
        return self.add(lambda e: e.copy_predicated(out, mask, data), wait)

    def scan(self, out, d0, d1, op0, op1, wait=()):
        return self.add(lambda e: e.tensor_tensor_scan(out, d0, d1, 0.0, op0, op1), wait)

    def mm(self, out, lhsT, rhs, start, stop, wait=(), mark=False):
        return self.add(lambda e: e.matmul(out, lhsT, rhs, start=start, stop=stop, skip_group_check=True), wait, mark)

    def turn(self, out, in_, ident, wait=(), mark=False):
        return self.add(lambda e: e.transpose(out, in_, ident), wait, mark)


class Buffer:
    def __init__(self, ap, sem=None):
        self.ap, self.free, self.sem, self.loads = ap, [], sem, 0


class Rotation:

    def __init__(self, buffers, free=()):
        self.idle = list(buffers)
        for b in self.idle:
            b.free = list(free)

    def take(self):
        return self.idle.pop(0)

    def give(self, buffer, *marks):
        buffer.free = list(marks)
        self.idle.append(buffer)


def build(nc, x, cols, fconst, iconst, lora_w, ctx, w_ada, w_in, w_out, w_ada2, w_hg, w_hgo, w_up, w_down, out):
    with ExitStack() as stack:
        def sb(name, shape, dt=F32, st=stack):
            return st.enter_context(nc.sbuf_tensor(name, shape, dt))

        def sem(name):
            return stack.enter_context(nc.semaphore(name))

        PE, DVE, AC, POOL, DMA = (Queue(sem(f"s_{n}")) for n in ("pe", "dve", "act", "pool", "sync"))
        psum = Rotation([Buffer(stack.enter_context(nc.psum_tensor(f"bank{i}", [P, BANK], F32))) for i in range(8)])

        def load(name, dst, src, wait=()):
            s = sem(name)
            DMA.wait(wait)
            DMA.program.append(lambda e: e.dma_start(dst, src).then_inc(s, 16))
            return (s, 16)

        colt = sb("colt", [P, NCOLS])
        fc = sb("fc", [P, len(FCONST) * P])
        ic = sb("ic", [P, len(ICONST) * P], I32)
        lora = sb("lora", [P, 4 * P])
        col_ld = load("ld_cols", colt[:], cols)
        fc_ld = load("ld_fc", fc[:], fconst)
        C = {n: fc[:, k * P:(k + 1) * P] for k, n in enumerate(FCONST)}
        M = {n: ic[:, k * P:(k + 1) * P] for k, n in enumerate(ICONST)}

        def col(name, k=0, n=1):
            at = COL_AT[name] + k
            return colt[:, at:at + n]

        small = sb("small", [P, 448])
        used = [0]

        def cells(n):
            used[0] += n
            assert used[0] <= 448
            return small[:, used[0] - n:used[0]]

        hT = sb("hT", [P, KT, SEQ])
        mixT = sb("mixT", [P, KT, SEQ])
        rows = sb("rows", [P, 2, D])
        gate_row = rows[:, 0, :]
        gain_row = rows[:, 1, :]
        ring = Rotation([Buffer(sb(f"w{i}", [P, D]), sem(f"ld_w{i}")) for i in range(4)])

        def weights(src, to=None):
            b = (to or ring).take()
            b.loads += 1
            DMA.wait(b.free)
            ap, s = b.ap, b.sem
            DMA.program.append(lambda e: e.dma_start(ap[:], src).then_inc(s, 16))
            return b, (b.sem, 16 * b.loads)

        one = cells(1)
        eps_n = cells(1)
        eps_gn = cells(1)
        cst = [POOL.fill(one, 1.0), POOL.fill(eps_n, NORM_EPS), POOL.fill(eps_gn, GN_EPS)]

        def sigmoid(out, in_, wait, bias=None):
            kw = {"bias": bias} if bias is not None else {}
            return AC.act(out, in_, ACT.Sigmoid, wait, **kw)

        def rsqrt(out, in_, wait, scale, eps):
            m = AC.act(out, in_, ACT.Ln, [*wait, *cst], scale=scale, bias=eps)
            return AC.act(out, out, ACT.Exp, [m], scale=-0.5)

        def silu_cols(name, n):
            t = cells(n)
            m = sigmoid(t, col(name, 0, n), [col_ld])
            return t, DVE.tt(t, t, col(name, 0, n), ALU.mult, [m])

        c_act, c_done = silu_cols("c", KT)
        c2_act = cells(2 * KT)
        c2v = c2_act.rearrange("p (k two) -> p k two", two=2)
        c2_done = []
        for n, name in enumerate(("c_2", "c_ctx_2")):
            m = sigmoid(c2v[:, :, n], col(name, 0, KT), [col_ld])
            c2_done.append(DVE.tt(c2v[:, :, n], c2v[:, :, n], col(name, 0, KT), ALU.mult, [m]))

        def modulation(dst, src, first, count, act, act_done, bias, n):
            bank = psum.take()
            for j in range(count):
                w, ld = weights(src[first + j])
                for k in range(KT):
                    done = PE.mm(bank.ap[:, n * j:n * j + n], w.ap[:, k * P:(k + 1) * P], act(k), k == 0, k == KT - 1,
                                 [ld, *act_done, *bank.free] if k == 0 else (), mark=(k == KT - 1))
                ring.give(w, done)
                if j % 4 == 3:
                    yield
            for i in range(n):
                m = DVE.tt(dst[:, i:n * count:n], bank.ap[:, i:n * count:n], col(bias, first, count), ALU.add,
                           [done, col_ld])
            psum.give(bank, m)
            modulated[dst_name(dst)] = m

        modulated = {}
        dst_names = []

        def dst_name(dst):
            for n, (d, k) in enumerate(dst_names):
                if d is dst:
                    return k
            raise KeyError

        def named(name, n):
            t = cells(n)
            dst_names.append((t, name))
            return t

        mod1 = named("mod1", 24)
        mod2a = named("mod2a", 32)
        mod2b = named("mod2b", 32)

        def broadcast_row(dst, column, wait, free):
            marks, dfree = [], []
            for k in range(KT):
                if k % 4 == 0:
                    bank = psum.take()
                dg = diag.take()
                m = DVE.ts(dg.ap[:], C["ident"], column(k), None, ALU.mult, wait=[*wait, fc_ld, *dg.free])
                done = PE.mm(bank.ap[:, (k % 4) * P:(k % 4 + 1) * P], C["ones"], dg.ap[:], True, True,
                             [m, fc_ld, *bank.free], mark=True)
                diag.give(dg, done)
                if k % 4 == 3:
                    m = DVE.copy(dst[:, (k // 4) * BANK:(k // 4 + 1) * BANK], bank.ap[:], [done, *free])
                    psum.give(bank, m)
            return m

        def gain_cols(dst, norm, scale, wait):
            return DVE.stt(dst, scale, 1.0, norm, ALU.add, ALU.mult, wait)

        def to_channels(xt, nt, rstd, ready, dst, gain, shift, mod_ready, tmp, dst_free):
            marks = []
            for g in range(0, nt, 4):
                n = min(4, nt - g)
                xs = []
                for t in range(g, g + n):
                    b = tmp.take()
                    m = AC.act(b.ap[:, 0:D], xt(t), ACT.Copy, [*ready(t), *b.free], scale=rstd(t))
                    xs.append((b, m))
                for k in range(KT):
                    bank = psum.take()
                    for i, (b, m) in enumerate(xs):
                        done = PE.turn(bank.ap[:, i * P:(i + 1) * P], b.ap[:, k * P:(k + 1) * P], C["ident"],
                                       [m, fc_ld, *bank.free], mark=(i == n - 1))
                    m = DVE.ts(dst[:, k, g * P:(g + n) * P], bank.ap[:, 0:n * P], gain[:, k:k + 1], shift(k),
                               ALU.mult, ALU.add, [done, *mod_ready, *dst_free])
                    psum.give(bank, m)
                for b, _ in xs:
                    tmp.give(b, done)
                marks.append(m)
            return marks[-1]

        def project(w, ld, src, ready, n=SEQ):
            banks = []
            for t in range(0, n, BANK):
                bank = psum.take()
                width = min(BANK, n - t)
                for k in range(KT):
                    done = PE.mm(bank.ap[:, 0:width], w.ap[:, k * P:(k + 1) * P], src[:, k, t:t + width],
                                 k == 0, k == KT - 1, [ld, *ready, *bank.free] if k == 0 else (), mark=(k == KT - 1))
                banks.append((bank, done, t, width))
            ring.give(w, done)
            return banks

        def project_tokens(w, ld, src, ready, nt=TT):
            banks = []
            for g in range(0, nt, 4):
                bank = psum.take()
                n = min(4, nt - g)
                for i in range(n):
                    for k in range(KT):
                        done = PE.mm(bank.ap[:, i * P:(i + 1) * P], src[:, k, (g + i) * P:(g + i + 1) * P],
                                     w.ap[:, k * P:(k + 1) * P], k == 0, k == KT - 1,
                                     [ld, *ready, *bank.free] if k == 0 else (), mark=(k == KT - 1 and i == n - 1))
                banks.append((bank, done, g * P, n * P))
            ring.give(w, done)
            return banks

        def head_sums(mat, src, ready):
            banks = []
            for t in range(NB):
                bank = psum.take()
                done = PE.mm(bank.ap[:], mat, src[:, t * BANK:(t + 1) * BANK], True, True,
                             [*ready, fc_ld, *bank.free], mark=True)
                banks.append((bank, done, t * BANK, BANK))
            return banks

        def run(*gens):
            live = list(gens)
            while live:
                for g in list(live):
                    for _ in range(g[1]):
                        try:
                            next(g[0])
                        except StopIteration:
                            live.remove(g)
                            break

        def flat(bank_marks):
            return [m for m in bank_marks]

        stats = cells(64)
        with ExitStack() as st:
            tiles = Rotation([Buffer(sb(f"tile{i}", [P, SEQ + 2], st=st)) for i in range(14)])
            half = Rotation([Buffer(sb(f"half{i}", [P, BANK], st=st)) for i in range(6)])
            lt_buf = [Buffer(sb(f"ltb{h}", [P, BANK], st=st)) for h in range(2)]
            mt_buf = [Buffer(sb(f"mtb{h}", [P, BANK], st=st)) for h in range(2)]
            rb_buf = [Buffer(sb(f"rbb{h}", [P, BANK], st=st)) for h in range(2)]
            rk_buf = [Buffer(sb(f"rkb{h}", [P, BANK], st=st)) for h in range(2)]
            t_buf = [Buffer(sb(f"tb{h}", [P, BANK], st=st)) for h in range(2)]
            tt_buf = [Buffer(sb(f"ttb{h}", [P, BANK], st=st)) for h in range(2)]
            u_buf = [Buffer(sb(f"ub{h}", [P, BANK], st=st)) for h in range(2)]
            xbuf = Rotation([Buffer(sb(f"xb{i}", [P, P], st=st)) for i in range(3)])
            state = Buffer(sb("state", [P, P], st=st))
            state_sum = Buffer(sb("state_sum", [P, P], st=st))
            zeroed = [POOL.fill(b.ap[:], 0.0) for b in (*lt_buf, *mt_buf, *rb_buf, *rk_buf)]

            in_chunk = sb("in_chunk", [P, SEQ], BF16, st=st)
            m = POOL.fill(in_chunk[:], 1.0)
            start_done = POOL.fill(in_chunk[:, 0:SEQ:P], 0.0, [m])

            xt, x_ld = [], []
            for t in range(TT):
                b = tiles.take()
                xt.append(b)
                x_ld.append(load(f"ld_x{t}", b.ap[:, 0:D], x[t * P:(t + 1) * P, :]))
            ic_ld = load("ld_ic", ic[:], iconst)
            lora_ld = load("ld_lora", lora[:], lora_w)
            sq = tiles.take()
            marks = []
            m = None
            for t in range(TT):
                m = AC.act(sq.ap[:, 0:D], xt[t].ap[:, 0:D], ACT.Square, [x_ld[t]] + ([m] if m else []),
                           accum_out=stats[:, t:t + 1])
            tiles.give(sq, m)
            rstd_done = rsqrt(stats[:, 0:TT], stats[:, 0:TT], [m], 1.0 / D, eps_n)
            for _ in modulation(mod1, w_ada, 0, 24, lambda k: c_act[:, k:k + 1], [c_done], "ada_b", 1):
                pass
            gain1 = cells(KT)
            g1 = gain_cols(gain1, col("norm_g", 0, KT), mod1[:, 8:16], [modulated["mod1"], col_ld])
            h_done = to_channels(lambda t: xt[t].ap[:, 0:D], TT, lambda t: stats[:, t:t + 1],
                                 lambda t: [rstd_done], hT, gain1, lambda k: mod1[:, k:k + 1], [g1],
                                 tiles, [])
            for b in xt:
                tiles.give(b, *AC.last())

            par_done = []
            keep_mu = cells(13)
            omka = cells(4)
            par_done.append(DVE.ts(keep_mu, col("mu", 0, 13), -1.0, 1.0, ALU.mult, ALU.add, [col_ld]))
            par_done.append(DVE.ts(omka, col("k_a", 0, 4), -1.0, 1.0, ALU.mult, ALU.add))
            decay_cols = cells(16)

            def shifted(ct):
                w, ld = weights(w_in[ct])
                raw, dst = tiles.take(), tiles.take()
                z = DVE.fill(raw.ap[:, 0:1], 0.0, raw.free)
                for bank, done, t, width in project(w, ld, hT, [h_done]):
                    m = AC.act(raw.ap[:, 1 + t:1 + t + width], bank.ap[:, 0:width], ACT.Copy, [done, *raw.free])
                    psum.give(bank, m)
                a = DVE.ts(dst.ap[:, 0:SEQ], raw.ap[:, 1:SEQ + 1], keep_mu[:, ct:ct + 1], None, ALU.mult,
                           wait=[m, *par_done, *dst.free])
                b = DVE.stt(dst.ap[:, 0:SEQ], raw.ap[:, 0:SEQ], col("mu", ct), dst.ap[:, 0:SEQ], ALU.mult, ALU.add,
                            [a, z])
                tiles.give(raw, b)
                return dst, b

            def silu_gate(ct, k):
                w, ld = weights(w_in[ct])
                for bank, done, t, width in project(w, ld, hT, [h_done]):
                    dst = mixT[:, k, t:t + width]
                    m = sigmoid(dst, bank.ap[:, 0:width], [done])
                    m = DVE.tt(dst, dst, bank.ap[:, 0:width], ALU.mult, [m])
                    psum.give(bank, m)
                return m

            def to_tokens(src, ready):
                dst = tiles.take()
                for g in range(NB):
                    bank = psum.take()
                    for i in range(4):
                        at = (4 * g + i) * P
                        done = PE.turn(bank.ap[:, i * P:(i + 1) * P], src[:, at:at + P], C["ident"],
                                       [*ready, *bank.free], mark=(i == 3))
                    m = AC.act(dst.ap[:, g * BANK:(g + 1) * BANK], bank.ap[:], ACT.Copy, [done, *dst.free])
                    psum.give(bank, m)
                return dst, m, done

            zt, z_done = shifted(IN_Z)
            z_done = [z_done, AC.act(zt.ap[0:HD, 0:SEQ], zt.ap[0:HD, 0:SEQ], ACT.Tanh, [z_done])]

            def rwkv():
                full = lambda b: b.ap[:, 0:SEQ]
                chunks = lambda ap: ap.rearrange("p (c t) -> p c t", t=P)
                for ht in range(4):
                    rT, r_done = shifted(IN_R + ht)
                    yield
                    kT, k_done = shifted(IN_K + ht)
                    yield
                    vT, v_done = shifted(IN_V + ht)
                    yield
                    gate_done = silu_gate(IN_G + ht, ht)
                    yield
                    mneg, aT = tiles.take(), tiles.take()
                    for dst, lo, base in ((mneg, 0, "w0"), (aT, HD, "a0")):
                        for t in range(NB):
                            bank = psum.take()
                            done = PE.mm(bank.ap[:], lora[lo:lo + HD, ht * P:(ht + 1) * P],
                                         zt.ap[lo:lo + HD, t * BANK:(t + 1) * BANK], True, True,
                                         [*z_done, lora_ld, *bank.free], mark=True)
                            a_done = sigmoid(dst.ap[:, t * BANK:(t + 1) * BANK], bank.ap[:],
                                             [done, col_ld, *dst.free], col(base, ht))
                            psum.give(bank, a_done)
                    decay_done = DVE.ts(full(mneg), full(mneg), math.exp(-0.5), None, ALU.mult, wait=[a_done])
                    yield
                    kk = tiles.take()
                    m = AC.act(full(kk), full(kT), ACT.Square, [k_done, col_ld, *kk.free], scale=col("k_k", ht))
                    sums = head_sums(C["pair_ones"], full(kk), [m])
                    for bank, done, t, width in sums:
                        m = DVE.ts(kk.ap[:, t:t + width], bank.ap[:], 1e-24, None, ALU.max, wait=[done, sums[-1][1]])
                        psum.give(bank, m)
                    m = AC.act(full(kk), full(kk), ACT.Ln, [m])
                    m = AC.act(full(kk), full(kk), ACT.Exp, [m], scale=-0.5)
                    kk_done = DVE.stt(full(kk), full(kT), col("k_k", ht), full(kk), ALU.mult, ALU.mult, [m])
                    tmp = tiles.take()
                    m = DVE.ts(full(tmp), full(aT), col("k_a", ht), omka[:, ht:ht + 1], ALU.mult, ALU.add,
                               [a_done, *tmp.free])
                    k_done = DVE.tt(full(kT), full(kT), full(tmp), ALU.mult, [m, kk_done])
                    a_done = DVE.tt(full(aT), full(kk), full(aT), ALU.mult, [m, kk_done])
                    m = DVE.stt(full(tmp), full(rT), col("r_k", ht), full(kT), ALU.mult, ALU.mult, [k_done, r_done])
                    bonus = tiles.take()
                    for bank, done, t, width in head_sums(C["pair_ones"], full(tmp), [m]):
                        m = DVE.tt(bonus.ap[:, t:t + width], bank.ap[:], vT.ap[:, t:t + width], ALU.mult,
                                   [done, v_done, *bonus.free])
                        psum.give(bank, m)
                    bonus_done = m
                    vtok, vtok_done, vT_read = to_tokens(full(vT), [v_done, fc_ld])
                    tiles.give(vT, bonus_done, vT_read)
                    yield
                    b = tiles.take()
                    m = DVE.scan(full(b), in_chunk[:], full(mneg), ALU.mult, ALU.subtract, [decay_done, start_done, *b.free])
                    bc = chunks(full(b))
                    mid, end = bc[:, :, P // 2 - 1], bc[:, :, P - 1]
                    dc = decay_cols[:, 0:TT]
                    m2 = DVE.tt(dc, end, mid, ALU.subtract, [m, *decay_free])
                    m2 = DVE.tt(dc[:, 0:TT - 1], dc[:, 0:TT - 1], bc[:, 1:TT, P // 2 - 1], ALU.add, [m2])
                    dc_done = AC.act(dc, dc, ACT.Exp, [m2])
                    from_mid = DVE.tt(chunks(full(tmp)), bc, bc[:, :, P // 2 - 1:P // 2].broadcast_to([P, TT, P]),
                                      ALU.subtract, [m, done])
                    up_done = AC.act(full(b), full(tmp), ACT.Exp, [from_mid, m2])
                    r_done = DVE.tt(full(rT), full(rT), full(b), ALU.mult, [up_done, m])
                    down_done = AC.act(full(b), full(tmp), ACT.Exp, [r_done], scale=-1.0)
                    k_done = DVE.tt(full(kT), full(kT), full(b), ALU.mult, [down_done])
                    b_done = DVE.tt(full(aT), full(aT), full(b), ALU.mult, [down_done, a_done])
                    m = DVE.tt(full(tmp), full(tmp), full(mneg), ALU.add, [down_done])
                    before_done = AC.act(full(tmp), full(tmp), ACT.Exp, [m])
                    a2_done = DVE.stt(full(kk), full(kk), -1.0, full(tmp), ALU.mult, ALU.mult, [before_done])
                    tiles.give(b, k_done, b_done)
                    tiles.give(tmp, a2_done)
                    tiles.give(mneg, m)
                    yield
                    ktok, ktok_done, _ = to_tokens(full(kT), [k_done])
                    btok, btok_done, _ = to_tokens(full(aT), [b_done])
                    yt = tiles.take()
                    y_marks = []
                    A, B, K, R = kk, aT, kT, rT
                    st_mark = DVE.fill(state.ap[:], 0.0, state.free)
                    yield
                    for hf in range(2):
                        at = lambda i: slice((4 * hf + i) * P, (4 * hf + i + 1) * P)
                        level_done = [None, None]
                        made = {}
                        for h in range(2):
                            rows = slice(h * HD, (h + 1) * HD)
                            rep = lambda mask: mask.rearrange("p (o t) -> p o t", o=1).broadcast_to([P, 4, P])
                            quad = lambda ap: ap.rearrange("p (c t) -> p c t", t=P)
                            ti = POOL.copy(quad(t_buf[h].ap[:]), rep(C["ident"]), [fc_ld, *t_buf[h].free])
                            tti = POOL.copy(quad(tt_buf[h].ap[:]), rep(C["ident"]), [*tt_buf[h].free])
                            for name, left, right, buf, mask in (
                                    ("LT", B, A, lt_buf[h], "lt"), ("L", A, B, None, "low1"),
                                    ("MT", K, A, mt_buf[h], "lt"), ("RB", B, R, rb_buf[h], "le"),
                                    ("RK", K, R, rk_buf[h], "le")):
                                bank = psum.take()
                                for i in range(4):
                                    done = PE.mm(bank.ap[:, i * P:(i + 1) * P], left.ap[rows, at(i)],
                                                 right.ap[rows, at(i)], True, True,
                                                 [a2_done, b_done, k_done, r_done, *bank.free], mark=(i == 3))
                                if name == "L":
                                    t_done = DVE.select(quad(t_buf[h].ap[:]), rep(M["low1"]), quad(bank.ap[:]),
                                                        [done, ti, ic_ld])
                                    psum.give(bank, t_done)
                                    continue
                                made[name, h] = DVE.select(quad(buf.ap[:]), rep(M[mask]), quad(bank.ap[:]),
                                                           [done, ic_ld, *zeroed, *buf.free])
                                psum.give(bank, made[name, h])
                                if name == "LT":
                                    tt_done = DVE.select(quad(tt_buf[h].ap[:]), rep(M["up1"]), quad(buf.ap[:]),
                                                         [made[name, h], tti])
                            level_done[h] = [t_done, tt_done, made["LT", h]]
                            yield
                        for n in (2, 4, 8, 16, 32, 64):
                            for h in range(2):
                                bank = psum.take()
                                for i in range(4):
                                    s = slice(i * P, (i + 1) * P)
                                    done = PE.mm(bank.ap[:, s], lt_buf[h].ap[:, s], t_buf[h].ap[:, s], True, True,
                                                 [*level_done[h], *bank.free], mark=(i == 3))
                                u_done = AC.act(u_buf[h].ap[:], bank.ap[:], ACT.Copy, [done, *u_buf[h].free])
                                psum.give(bank, u_done)
                                level_done[h] = [u_done, *level_done[h]]
                                lt_read = done
                            yield
                            for h in range(2):
                                marks = []
                                if n < 64:
                                    bank = psum.take()
                                    for i in range(4):
                                        s = slice(i * P, (i + 1) * P)
                                        done = PE.mm(bank.ap[:, s], tt_buf[h].ap[:, s], u_buf[h].ap[:, s], True, True,
                                                     [*level_done[h], *bank.free], mark=(i == 3))
                                    tb, t_wait = bank, done
                                bank = psum.take()
                                for i in range(4):
                                    s = slice(i * P, (i + 1) * P)
                                    done = PE.mm(bank.ap[:, s], u_buf[h].ap[:, s], tt_buf[h].ap[:, s], True, True,
                                                 [*level_done[h], *bank.free], mark=(i == 3))
                                u_buf[h].free = [done]
                                if n < 64:
                                    m = DVE.select(quad(t_buf[h].ap[:]), rep(M[f"low{n}"]), quad(tb.ap[:]), [t_wait])
                                    psum.give(tb, m)
                                    marks.append(m)
                                m = DVE.select(quad(tt_buf[h].ap[:]), rep(M[f"up{n}"]), quad(bank.ap[:]), [done])
                                psum.give(bank, m)
                                level_done[h] = [*marks, m]
                            yield
                        for h in range(2):
                            lt_buf[h].free = [lt_read]
                            t_buf[h].free = [lt_read]
                        for i in range(4):
                            c = 4 * hf + i
                            s = slice(i * P, (i + 1) * P)
                            bank = psum.take()
                            PE.mm(bank.ap[:, 0:P], A.ap[:, at(i)], state.ap[:], True, False, [st_mark, *bank.free])
                            for h in range(2):
                                hc = slice(h * HD, (h + 1) * HD)
                                done = PE.mm(bank.ap[:, hc], mt_buf[h].ap[:, s], vtok.ap[:, c * P + h * HD:c * P + (h + 1) * HD],
                                             False, True, [made["MT", h], vtok_done], mark=(h == 1))
                            xs = xbuf.take()
                            x_done = DVE.copy(xs.ap[:], bank.ap[:, 0:P], [done, *xs.free])
                            psum.give(bank, x_done)
                            yb, sbk = psum.take(), psum.take()
                            PE.mm(yb.ap[:, 0:P], state.ap[:], R.ap[:, at(i)], True, False, yb.free)
                            for h in range(2):
                                hc = slice(h * HD, (h + 1) * HD)
                                PE.mm(yb.ap[hc, 0:P], vtok.ap[:, c * P + h * HD:c * P + (h + 1) * HD], rk_buf[h].ap[:, s],
                                      False, False, [made["RK", h]])
                            PE.mm(sbk.ap[:, 0:P], ktok.ap[:, c * P:(c + 1) * P], vtok.ap[:, c * P:(c + 1) * P], True, False,
                                  [ktok_done, *sbk.free])
                            bank = psum.take()
                            for h in range(2):
                                hc = slice(h * HD, (h + 1) * HD)
                                done = PE.mm(bank.ap[:, hc], tt_buf[h].ap[:, s], xs.ap[:, hc], True, True,
                                             [x_done, *level_done[h], *bank.free], mark=(h == 1))
                            xbuf.give(xs, done)
                            sa = xbuf.take()
                            sa_done = DVE.copy(sa.ap[:], bank.ap[:, 0:P], [done, *sa.free])
                            psum.give(bank, sa_done)
                            st_read = PE.mm(sbk.ap[:, 0:P], btok.ap[:, c * P:(c + 1) * P], sa.ap[:], False, True,
                                            [sa_done, btok_done], mark=True)
                            m = DVE.tt(state_sum.ap[:], sbk.ap[:, 0:P], state.ap[:], ALU.add, [st_read])
                            st_mark = DVE.stt(state.ap[:], state_sum.ap[:], dc[:, c:c + 1], C["pair_ones"],
                                              ALU.mult, ALU.mult, [m, dc_done])
                            psum.give(sbk, m)
                            for h in range(2):
                                hc = slice(h * HD, (h + 1) * HD)
                                done = PE.mm(yb.ap[hc, 0:P], sa.ap[:, hc], rb_buf[h].ap[:, s], False, True,
                                             [made["RB", h]], mark=(h == 1))
                            xbuf.give(sa, done)
                            y_done = AC.act(yt.ap[:, at(i)], yb.ap[:, 0:P], ACT.Copy, [done, *yt.free])
                            psum.give(yb, y_done)
                            yield
                        for h in range(2):
                            for bf in (mt_buf, rb_buf, rk_buf, tt_buf):
                                bf[h].free = [done]
                    state.free = [done]
                    decay_free[:] = [st_mark]
                    for bf in (A, B, K, R, ktok, btok, vtok):
                        tiles.give(bf, done)
                    tmp = tiles.take()
                    for bank, done, t, width in head_sums(C["pair_ones"], full(yt), [y_done]):
                        m = DVE.stt(yt.ap[:, t:t + width], bank.ap[:], -1.0 / HD, yt.ap[:, t:t + width],
                                    ALU.mult, ALU.add, [done])
                        psum.give(bank, m)
                    m = AC.act(full(tmp), full(yt), ACT.Square, [m, *tmp.free])
                    sums = head_sums(C["pair_ones"], full(tmp), [m])
                    for bank, done, t, width in sums:
                        m = rsqrt(tmp.ap[:, t:t + width], bank.ap[:], [done, sums[-1][1]], 1.0 / HD, eps_gn)
                        psum.give(bank, m)
                    m = DVE.tt(full(yt), full(yt), full(tmp), ALU.mult, [m])
                    tiles.give(tmp, m)
                    m = DVE.ts(full(yt), full(yt), col("ln_w", ht), col("ln_b", ht), ALU.mult, ALU.add, [m])
                    m = DVE.tt(full(yt), full(yt), full(bonus), ALU.add, [m, bonus_done])
                    m = DVE.tt(mixT[:, ht, :], mixT[:, ht, :], full(yt), ALU.mult, [m, gate_done])
                    tiles.give(yt, m)
                    tiles.give(bonus, m)
                    mix_done.append(m)
                    yield

            decay_free = []
            mix_done = []

            def stick():
                for ht in range(4):
                    qk = []
                    for ct, scale in ((SB_Q, HD ** -0.5), (SB_K, 1.0)):
                        w, ld = weights(w_in[ct + ht])
                        dst = tiles.take()
                        for bank, done, t, width in project(w, ld, hT, [h_done]):
                            m = AC.act(dst.ap[:, t:t + width], bank.ap[:], ACT.Copy, [done, *dst.free], scale=scale)
                            psum.give(bank, m)
                        qk.append((dst, m))
                        yield
                    (qT, q_done), (kT, k_done) = qk
                    w, ld = weights(w_in[SB_V + ht])
                    v = tiles.take()
                    for bank, done, t, width in project_tokens(w, ld, hT, [h_done]):
                        v_done = AC.act(v.ap[:, t:t + width], bank.ap[:], ACT.Copy, [done, *v.free])
                        psum.give(bank, v_done)
                    yield
                    gate_done = silu_gate(SB_G + ht, 4 + ht)
                    yield
                    ot = tiles.take()
                    for qh in range(2):
                        top = 4 * qh + 3
                        obank = psum.take()
                        acc = [psum.take(), psum.take()]
                        acc_read = [[], []]
                        for kb in range(top, -1, -1):
                            q0 = max(kb * P, qh * BANK)
                            o, width = q0 - qh * BANK, qh * BANK + BANK - q0
                            on_diag = kb >= 4 * qh
                            for h in range(2):
                                rows = slice(h * HD, (h + 1) * HD)
                                zb = psum.take()
                                done = PE.mm(zb.ap[:, 0:width], kT.ap[rows, kb * P:(kb + 1) * P],
                                             qT.ap[rows, q0:q0 + width], True, True,
                                             [q_done, k_done, *zb.free], mark=True)
                                z, w1 = half.take(), half.take()
                                zs, ws = z.ap[:, 0:width], w1.ap[:, 0:width]
                                z_done = AC.act(zs, zb.ap[:, 0:width], ACT.Copy, [done, *z.free])
                                psum.give(zb, z_done)
                                m = DVE.stt(ws, zs, -1.0, zs, ALU.mult, ALU.max, [z_done, *w1.free])
                                m = AC.act(ws, ws, ACT.Exp, [m], scale=-1.0)
                                m = AC.act(ws, ws, ACT.Ln, [m, *cst], bias=one)
                                sp = DVE.stt(ws, zs, 0.0, ws, ALU.max, ALU.add, [m])
                                if on_diag:
                                    sp = DVE.tt(ws[:, 0:P], ws[:, 0:P], C["key_before_query"], ALU.mult, [sp, fc_ld])
                                ab = acc[h].ap[:, o:o + width]
                                s_done = PE.mm(ab, C["at_or_after"], ws, kb == top, kb == 0,
                                               [sp, *acc_read[h], *acc[h].free], mark=True)
                                m = DVE.tt(zs, zs, ab, ALU.subtract, [s_done])
                                acc_read[h] = [m]
                                if kb > 0:
                                    done = PE.mm(ab, C["before"], ws, False, False, [m], mark=True)
                                    half.give(w1, done)
                                else:
                                    half.give(w1, s_done)
                                    psum.give(acc[h], m)
                                if on_diag:
                                    m = DVE.ts(zs[:, 0:P], zs[:, 0:P], 0.0, None, ALU.min, wait=[m])
                                m = AC.act(zs, zs, ACT.Exp, [m])
                                if on_diag:
                                    m = DVE.tt(zs[:, 0:P], zs[:, 0:P], C["key_before_query"], ALU.mult, [m])
                                done = PE.mm(obank.ap[rows, o:o + width], v.ap[:, kb * P + h * HD:kb * P + (h + 1) * HD], zs,
                                             kb == top, kb == 0, [m, v_done, *obank.free], mark=True)
                                half.give(z, done)
                                yield
                        m = AC.act(ot.ap[:, qh * BANK:(qh + 1) * BANK], obank.ap[:], ACT.Copy, [done, *ot.free])
                        psum.give(obank, m)
                    for bf in (qT, kT, v):
                        tiles.give(bf, done)
                    tmp = tiles.take()
                    m = AC.act(tmp.ap[:, 0:SEQ], ot.ap[:, 0:SEQ], ACT.Square, [m, *tmp.free])
                    sums = head_sums(C["pair_ones"], tmp.ap[:, 0:SEQ], [m])
                    for bank, done, t, width in sums:
                        m = rsqrt(tmp.ap[:, t:t + width], bank.ap[:], [done, sums[-1][1]], 1.0 / HD, eps_n)
                        psum.give(bank, m)
                    m = DVE.stt(ot.ap[:, 0:SEQ], ot.ap[:, 0:SEQ], col("sb_g", ht), tmp.ap[:, 0:SEQ], ALU.mult, ALU.mult, [m])
                    tiles.give(tmp, m)
                    gate = mixT[:, 4 + ht, :].rearrange("p (q b) -> p q b", b=TT)
                    m = DVE.tt(gate, gate, ot.ap[:, 0:SEQ].rearrange("p (b q) -> p q b", b=TT), ALU.mult, [m, gate_done])
                    tiles.give(ot, m)
                    mix_done.append(m)
                    yield

            def second_modulation():
                yield from modulation(mod2a, w_ada2, 0, 16, lambda k: c2v[:, k, :], c2_done, "b_ada_2", 2)
                yield from modulation(mod2b, w_ada2, 16, 32, lambda k: c2v[:, k, 0:1], c2_done, "b_ada_2", 1)

            run((rwkv(), 1), (stick(), 1), (second_modulation(), 1))

        phase = lambda: [*PE.last(), *DVE.last(), *AC.last(), *POOL.last()]

        def residual_tile(xr, t, banks, ready):
            for half_i, (bank, done) in enumerate(banks):
                s = slice(half_i * BANK, (half_i + 1) * BANK)
                tmp = prod.take()
                m = DVE.tt(tmp.ap[:], bank.ap[:], gate_row[:, s], ALU.mult, [done, *ready, *tmp.free])
                psum.give(bank, m)
                m = DVE.tt(xr[:, t, s], xr[:, t, s], tmp.ap[:], ALU.add, [m])
                prod.give(tmp, m)
            return m

        def output_product(src, ws, tile_of, nk, t, ready):
            banks = []
            for hf in range(2):
                bank = psum.take()
                for k in range(nk):
                    done = PE.mm(bank.ap[:], tile_of(k)[:, t * P:(t + 1) * P],
                                 ws[k][0].ap[:, hf * BANK:(hf + 1) * BANK], k == 0, k == nk - 1,
                                 [ws[k][1], *bank.free, *ready], mark=(k == nk - 1))
                banks.append((bank, done))
            return banks

        with ExitStack() as st:
            p1 = phase()
            X = sb("X", [P, TT, D], st=st)
            diag = Rotation([Buffer(sb(f"diag{i}", [P, P], st=st)) for i in range(2)], p1)
            prod = Rotation([Buffer(sb(f"prod{i}", [P, BANK], st=st)) for i in range(2)], p1)

            def out_slots(scope, name, marks):
                return Rotation([Buffer(sb(f"{name}{i}", [P, D], st=scope), sem(f"ld_{name}{i}")) for i in range(6)], marks)

            x2_ld = [load(f"ld_xr{t}", X[:, t, :], x[t * P:(t + 1) * P, :], p1) for t in range(TT)]

            def out_weights(src, n, oring):
                got = []
                for k in range(n):
                    r = oring if oring.idle else ring
                    w, ld = weights(src[k], r)
                    got.append((w, ld, r))
                return got

            def release(ws, mark):
                for w, _, r in ws:
                    r.give(w, mark)

            g_done = broadcast_row(gate_row, lambda k: mod1[:, 16 + k:17 + k], [modulated["mod1"]], [])
            f_done = broadcast_row(gain_row, lambda k: col("final_g", k), [col_ld], [])
            sq = sb("sq", [P, D], BF16, st=st)
            so = ExitStack()
            ws = out_weights(w_out, KT, out_slots(so, "ow", p1))
            ss = cells(2 * TT)
            n_done = []
            m_sq = None
            for t in range(TT):
                banks = output_product(mixT, ws, lambda k: mixT[:, k, :], KT, t, mix_done)
                m = residual_tile(X, t, banks, [g_done, x2_ld[t]])
                m_sq = AC.act(sq[:], X[:, t, :], ACT.Square, [m, *p1, *([m_sq] if m_sq else [])],
                              accum_out=ss[:, t:t + 1])
                m = rsqrt(ss[:, t:t + 1], ss[:, t:t + 1], [m_sq], 1.0 / D, eps_n)
                m = DVE.stt(X[:, t, :], X[:, t, :], ss[:, t:t + 1], gain_row, ALU.mult, ALU.mult, [m, f_done])
                m_sq = AC.act(sq[:], X[:, t, :], ACT.Square, [m, m_sq], accum_out=ss[:, TT + t:TT + t + 1])
                n_done.append(rsqrt(ss[:, TT + t:TT + t + 1], ss[:, TT + t:TT + t + 1], [m_sq], 1.0 / D, eps_n))
            release(ws, banks[-1][1])
            so.close()
            p1 = phase()

            lb, lbt = cells(16), cells(32)
            l0, l1 = col("lb_logits", 0, 16), col("lb_logits", 16, 16)
            e0, mx = lbt[:, 0:16], lbt[:, 16:32]
            m = DVE.tt(mx, l0, l1, ALU.max, [col_ld])
            m2 = DVE.tt(e0, l0, mx, ALU.subtract, [m])
            m = DVE.tt(mx, l1, mx, ALU.subtract, [m2])
            m = AC.act(lbt[:], lbt[:], ACT.Exp, [m])
            m = DVE.tt(mx, e0, mx, ALU.add, [m])
            m = DVE.add(lambda e: e.reciprocal(mx, mx), [m])
            lb_done = DVE.tt(lb, e0, mx, ALU.mult, [m])
            omlb = cells(16)
            lb_done = DVE.ts(omlb, lb, -1.0, 1.0, ALU.mult, ALU.add, [lb_done])

            with ExitStack() as sh:
                tiles = Rotation([Buffer(sb(f"ht{i}", [P, SEQ + 2], st=sh)) for i in range(7)], p1)
                hcT = sb("hcT", [P, KT, CTX], st=sh)
                cst_t = Rotation([Buffer(sb(f"cx{i}", [P, CTX], st=sh)) for i in range(3)], p1)
                m2a = mod2a.rearrange("p (k two) -> p k two", two=2)
                gain_l, gain_c = cells(KT), cells(KT)
                gl = gain_cols(gain_l, col("norm_g_2", 0, KT), m2a[:, 8:16, 0], [modulated["mod2a"]])
                gc = gain_cols(gain_c, col("norm_g_2", 0, KT), m2a[:, 8:16, 1], [])
                cs = cells(2)
                cx = []
                for t in range(CTX // P):
                    b = tiles.take()
                    ld = load(f"ld_ctx{t}", b.ap[:, 0:D], ctx[t * P:(t + 1) * P, :], b.free)
                    m_sq = AC.act(sq[:], b.ap[:, 0:D], ACT.Square, [ld, m_sq], accum_out=cs[:, t:t + 1])
                    cx.append(b)
                c_rstd = rsqrt(cs, cs, [m_sq], 1.0 / D, eps_n)
                hc_done = to_channels(lambda t: cx[t].ap[:, 0:D], CTX // P, lambda t: cs[:, t:t + 1], lambda t: [c_rstd],
                                      hcT, gain_c, lambda k: m2a[:, k, 1:2], [gc], tiles, p1)
                for b in cx:
                    tiles.give(b, *AC.last())
                h_done = to_channels(lambda t: X[:, t, :], TT, lambda t: ss[:, TT + t:TT + t + 1], lambda t: [n_done[t]],
                                     hT, gain_l, lambda k: m2a[:, k, 0:1], [gl], tiles, p1)

                chunk_start = sb("chunk_start", [P, SEQ], BF16, st=sh)
                sc = sb("sc", [P, 2, SEQ], st=sh)
                states_hi = sb("states_hi", [P, SEQ // HG_CHUNK // 2, P], st=sh)
                states_lo = rows[:].rearrange("p a (c v) -> p (a c) v", v=P)

                def state_at(c):
                    n = SEQ // HG_CHUNK // 2
                    return states_lo[:, c, :] if c < n else states_hi[:, c - n, :]

                cs_done = POOL.fill(chunk_start[:], 1.0, p1)
                cs_done = POOL.fill(chunk_start[:, 0:SEQ:HG_CHUNK], 0.0, [cs_done])
                dcy = [cells(SEQ // HG_CHUNK) for _ in range(2)]
                sc_free, states_free, dcy_free = [[], []], [[], []], [[], []]

                def forget(ct, src, ready, n, d, h, pool):
                    w, ld = weights(w_hg[ct])
                    lf, k = pool.take(), pool.take()
                    j = d * 8 + h
                    for bank, done, t, width in project(w, ld, src, ready, n):
                        m = sigmoid(lf.ap[:, t:t + width], bank.ap[:, 0:width], [done, *lf.free])
                        psum.give(bank, m)
                    f = DVE.ts(lf.ap[:, 0:n], lf.ap[:, 0:n], omlb[:, j:j + 1], lb[:, j:j + 1], ALU.mult, ALU.add,
                               [m, lb_done])
                    k_done = DVE.ts(k.ap[:, 0:n], lf.ap[:, 0:n], -1.0, 1.0, ALU.mult, ALU.add, [f, *k.free])
                    lf_done = AC.act(lf.ap[:, 0:n], lf.ap[:, 0:n], ACT.Ln, [k_done])
                    return lf, lf_done, k, k_done

                def running(lf, ready, dst, n, d):
                    if d == 0:
                        return DVE.scan(dst.ap[:, 0:n], chunk_start[:, 0:n], lf.ap[:, 0:n], ALU.mult, ALU.add,
                                        [ready, cs_done, *dst.free])
                    return DVE.scan(dst.ap[:, 0:n][:, ::-1], chunk_start[:, 0:n], lf.ap[:, 0:n][:, ::-1],
                                    ALU.mult, ALU.add, [ready, cs_done, *dst.free])

                by_chunk = lambda ap: ap.rearrange("p (c t) -> p c t", t=HG_CHUNK)

                def to_end(b, ready, dst, k, k_done, n, d):
                    last = HG_CHUNK - 1 if d == 0 else 0
                    bc = by_chunk(b.ap[:, 0:n])
                    m = DVE.tt(by_chunk(dst.ap[:, 0:n]), bc[:, :, last:last + 1].broadcast_to([P, n // HG_CHUNK, HG_CHUNK]),
                               bc, ALU.subtract, [ready, *dst.free])
                    m = AC.act(dst.ap[:, 0:n], dst.ap[:, 0:n], ACT.Exp, [m])
                    return DVE.tt(dst.ap[:, 0:n], dst.ap[:, 0:n], k.ap[:, 0:n], ALU.mult, [m, k_done])

                def tokens_of(src, ready, dst, n):
                    for g in range(0, n // P, 4):
                        bank = psum.take()
                        w = min(4, n // P - g)
                        for i in range(w):
                            at = (g + i) * P
                            done = PE.turn(bank.ap[:, i * P:(i + 1) * P], src.ap[:, at:at + P], C["ident"],
                                           [ready, *bank.free], mark=(i == w - 1))
                        m = AC.act(dst.ap[:, g * P:(g + w) * P], bank.ap[:, 0:w * P], ACT.Copy, [done, *dst.free])
                        psum.give(bank, m)
                    return m, done

                def chunk_products(kd, kd_done, v, v_done, n, group):
                    for g in group:
                        banks = [psum.take() for _ in range(PER_TILE)]
                        span = min(4 * PER_TILE, n // HG_CHUNK - 4 * PER_TILE * g)
                        done = [None] * PER_TILE
                        for par in range(PER_TILE):
                            rws = slice(par * HG_CHUNK, (par + 1) * HG_CHUNK)
                            for i in range(span // PER_TILE):
                                at = (4 * g + i) * P
                                done[par] = PE.mm(banks[par].ap[:, i * P:(i + 1) * P], kd.ap[rws, at:at + P],
                                                  v.ap[rws, at:at + P], True, True,
                                                  [kd_done, v_done, *banks[par].free],
                                                  mark=(i == span // PER_TILE - 1))
                        yield g, banks, done, span

                def product_of(banks, c):
                    return banks[c % PER_TILE].ap[:, (c // PER_TILE) * P:(c // PER_TILE + 1) * P]

                def hgrn(h):
                    w, ld = weights(w_hg[HG_I + h])
                    vc = cst_t.take()
                    for bank, done, t, width in project_tokens(w, ld, hcT, [hc_done], CTX // P):
                        vc_done = AC.act(vc.ap[:, t:t + width], bank.ap[:, 0:width], ACT.Copy, [done, *vc.free])
                        psum.give(bank, vc_done)
                    w, ld = weights(w_hg[HG_I + h])
                    v = tiles.take()
                    for bank, done, t, width in project_tokens(w, ld, hT, [h_done]):
                        v_done = AC.act(v.ap[:, t:t + width], bank.ap[:], ACT.Copy, [done, *v.free])
                        psum.give(bank, v_done)
                    w, ld = weights(w_hg[HG_Q + h])
                    q = tiles.take()
                    for bank, done, t, width in project(w, ld, hT, [h_done]):
                        m = sigmoid(q.ap[:, t:t + width], bank.ap[:], [done, *q.free])
                        q_done = DVE.tt(q.ap[:, t:t + width], q.ap[:, t:t + width], bank.ap[:], ALU.mult, [m])
                        psum.give(bank, q_done)
                    obanks, o_open = None, []
                    for d in range(2):
                        sk = 0 if d == 0 else SEQ // HG_CHUNK - 1
                        lf, lf_done, k, k_done = forget(HG_F + 8 * d + h, hcT, [hc_done], CTX, d, h, cst_t_pool)
                        b = cst_t_pool.take()
                        m = running(lf, lf_done, b, CTX, d)
                        cst_t_pool.give(lf, m)
                        kd = cst_t_pool.take()
                        dc_at = by_chunk(b.ap[:, 0:CTX])[:, :, HG_CHUNK - 1 if d == 0 else 0]
                        cdec = dcy[d][:, 0:CTX // HG_CHUNK]
                        dec_done = AC.act(cdec, dc_at, ACT.Exp, [m, *dcy_free[d]])
                        kd_done = to_end(b, m, kd, k, k_done, CTX, d)
                        cst_t_pool.give(b, kd_done, dec_done)
                        cst_t_pool.give(k, kd_done)
                        kt = cst_t_pool.take()
                        kt_done, kd_read = tokens_of(kd, kd_done, kt, CTX)
                        cst_t_pool.give(kd, kd_read)
                        S = state_at(sk)
                        s_done = DVE.fill(S, 0.0, [*states_free[0], *p1])
                        for g, banks, done, span in chunk_products(kt, kt_done, vc, vc_done, CTX, [0]):
                            order = range(span) if d == 0 else range(span - 1, -1, -1)
                            for c in order:
                                s_done = DVE.stt(S, S, cdec[:, c:c + 1], product_of(banks, c),
                                                 ALU.mult, ALU.add, [*done, s_done, dec_done])
                            for bk in banks:
                                psum.give(bk, s_done)
                        cst_t_pool.give(kt, *done)
                        ctx_s = s_done
                        lf, lf_done, k, k_done = forget(HG_F + 8 * d + h, hT, [h_done], SEQ, d, h, tiles)
                        b = tiles.take()
                        b_done = running(lf, lf_done, b, SEQ, d)
                        bc = by_chunk(b.ap[:, 0:SEQ])
                        dec_done = AC.act(dcy[d], bc[:, :, HG_CHUNK - 1 if d == 0 else 0], ACT.Exp, [b_done, ctx_s])
                        kd_done = to_end(b, b_done, lf, k, k_done, SEQ, d)
                        kt = tiles.take()
                        kt_done, kd_read = tokens_of(lf, kd_done, kt, SEQ)
                        gr = [0, 1] if d == 0 else [1, 0]
                        for g, banks, done, span in chunk_products(kt, kt_done, v, v_done, SEQ, gr):
                            order = range(16 * g, 16 * g + 16) if d == 0 else range(16 * g + 15, 16 * g - 1, -1)
                            for c in order:
                                nx = c + 1 if d == 0 else c - 1
                                if not 0 <= nx < SEQ // HG_CHUNK:
                                    continue
                                i = c % 16
                                s_done = DVE.stt(state_at(nx), state_at(c), dcy[d][:, c:c + 1],
                                                 product_of(banks, i),
                                                 ALU.mult, ALU.add, [*done, s_done, dec_done])
                            for bk in banks:
                                psum.give(bk, s_done)
                        dcy_free[d] = [s_done]
                        ref = HG_CHUNK // 2 if d == 0 else HG_CHUNK // 2 - 1
                        m = DVE.tt(by_chunk(lf.ap[:, 0:SEQ]), bc,
                                   bc[:, :, ref:ref + 1].broadcast_to([P, SEQ // HG_CHUNK, HG_CHUNK]),
                                   ALU.subtract, [kd_read])
                        e1 = AC.act(kt.ap[:, 0:SEQ], lf.ap[:, 0:SEQ], ACT.Exp, [m, *done])
                        qe_done = DVE.stt(kt.ap[:, 0:SEQ], kt.ap[:, 0:SEQ], SCORE_SCALE, q.ap[:, 0:SEQ], ALU.mult, ALU.mult,
                                          [e1, q_done])
                        e2 = AC.act(lf.ap[:, 0:SEQ], lf.ap[:, 0:SEQ], ACT.Exp, [e1], scale=-1.0)
                        ke_done = DVE.tt(k.ap[:, 0:SEQ], k.ap[:, 0:SEQ], lf.ap[:, 0:SEQ], ALU.mult, [e2])
                        mask = C["hg_fwd" if d == 0 else "hg_bwd"].rearrange("p (o t) -> p o t", o=1).broadcast_to([P, 4, P])
                        quad = lambda ap: ap.rearrange("p (c t) -> p c t", t=P)
                        for g in range(2):
                            bank = psum.take()
                            for i in range(4):
                                at = slice((4 * g + i) * P, (4 * g + i + 1) * P)
                                done = PE.mm(bank.ap[:, i * P:(i + 1) * P], k.ap[:, at], kt.ap[:, at], True, True,
                                             [qe_done, ke_done, *bank.free], mark=(i == 3))
                            sc_done = DVE.stt(quad(sc[:, d, g * BANK:(g + 1) * BANK]), quad(bank.ap[:]), 1.0 / SCORE_SCALE,
                                              mask, ALU.mult, ALU.mult, [done, *p1, *sc_free[d]])
                            psum.give(bank, sc_done)
                        m = AC.act(b.ap[:, 0:SEQ], b.ap[:, 0:SEQ], ACT.Exp, [m, dec_done])
                        qb_done = DVE.tt(b.ap[:, 0:SEQ], b.ap[:, 0:SEQ], q.ap[:, 0:SEQ], ALU.mult, [m])
                        tiles.give(lf, ke_done)
                        tiles.give(k, done)
                        tiles.give(kt, done)
                        yield
                        if d == 0:
                            obanks = [psum.take(), psum.take()]
                        for p in range(TT):
                            ob = obanks[p // 4].ap[:, (p % 4) * P:(p % 4 + 1) * P]
                            fr = obanks[p // 4].free
                            PE.mm(ob, v.ap[:, p * P:(p + 1) * P], sc[:, d, p * P:(p + 1) * P],
                                  d == 0 and p % 4 == 0, False, [sc_done, *fr])
                            for c in range(PER_TILE * p, PER_TILE * (p + 1)):
                                done = PE.mm(ob[:, (c % PER_TILE) * HG_CHUNK:(c % PER_TILE + 1) * HG_CHUNK], state_at(c),
                                             b.ap[:, c * HG_CHUNK:(c + 1) * HG_CHUNK], False, d == 1 and p % 4 == 3,
                                             [s_done, qb_done], mark=(c % PER_TILE == PER_TILE - 1))
                        tiles.give(b, done)
                        sc_free[d] = [done]
                        states_free[0] = [done]
                    cst_t.give(vc, *PE.last())
                    tiles.give(v, done)
                    tiles.give(q, qb_done)
                    o, tmp = tiles.take(), tiles.take()
                    for g in range(2):
                        s = slice(g * BANK, (g + 1) * BANK)
                        m = AC.act(o.ap[:, s], obanks[g].ap[:], ACT.Copy, [done, *o.free])
                        psum.give(obanks[g], m)
                    m = AC.act(tmp.ap[:, 0:SEQ], o.ap[:, 0:SEQ], ACT.Square, [m, *tmp.free])
                    sums = head_sums(C["ones"], tmp.ap[:, 0:SEQ], [m])
                    for bank, done, t, width in sums:
                        m = rsqrt(tmp.ap[:, t:t + width], bank.ap[:], [done, sums[-1][1]], 1.0 / P, eps_n)
                        psum.give(bank, m)
                    o_done = DVE.stt(o.ap[:, 0:SEQ], o.ap[:, 0:SEQ], col("gnorm"), tmp.ap[:, 0:SEQ], ALU.mult, ALU.mult, [m])
                    tiles.give(tmp, o_done)
                    w, ld = weights(w_hg[HG_G + h])
                    for bank, done, t, width in project(w, ld, hT, [h_done]):
                        dst = mixT[:, h, t:t + width]
                        m = sigmoid(dst, bank.ap[:], [done, *p1])
                        m = DVE.tt(dst, dst, bank.ap[:], ALU.mult, [m])
                        psum.give(bank, m)
                    m = DVE.tt(mixT[:, h, :], mixT[:, h, :], o.ap[:, 0:SEQ], ALU.mult, [m, o_done])
                    tiles.give(o, m)
                    hg_mix.append(m)
                    yield

                cst_t_pool = Rotation([Buffer(sb(f"cp{i}", [P, CTX], st=sh)) for i in range(4)], p1)
                hg_mix = []
                for h in range(8):
                    run((hgrn(h), 1))

            p2 = phase()
            g_done = broadcast_row(gate_row, lambda k: mod2b[:, k:k + 1], [modulated["mod2b"]], p2)
            oring = out_slots(st, "fw", p2)
            ws = out_weights(w_hgo, KT, oring)
            n_done = []
            for t in range(TT):
                banks = output_product(mixT, ws, lambda k: mixT[:, k, :], KT, t, hg_mix)
                m = residual_tile(X, t, banks, [g_done, *p2])
                m_sq = AC.act(sq[:], X[:, t, :], ACT.Square, [m, m_sq], accum_out=ss[:, t:t + 1])
                n_done.append(rsqrt(ss[:, t:t + 1], ss[:, t:t + 1], [m_sq], 1.0 / D, eps_n))
            release(ws, banks[-1][1])

            with ExitStack() as sf:
                tiles = Rotation([Buffer(sb(f"ft{i}", [P, SEQ + 2], st=sf)) for i in range(6)], p2)
                acts = Rotation([Buffer(mixT[:, k, :]) for k in range(KT)], [banks[-1][1]])
                gain_f = cells(KT)
                gf = gain_cols(gain_f, col("norm_g_2", KT, KT), mod2b[:, 16:24], [modulated["mod2b"]])
                h_done = to_channels(lambda t: X[:, t, :], TT, lambda t: ss[:, t:t + 1], lambda t: [n_done[t]],
                                     hT, gain_f, lambda k: mod2b[:, 8 + k:9 + k], [gf], tiles, p2)
                x_read = AC.last()
                g_done = broadcast_row(gate_row, lambda k: mod2b[:, 24 + k:25 + k], [modulated["mod2b"]], [m])
                f_done = broadcast_row(gain_row, lambda k: col("final_g_2", k), [col_ld], p2)

                def convolved(j):
                    w, ld = weights(w_up[j])
                    raw, dst = tiles.take(), tiles.take()
                    z = DVE.fill(raw.ap[:, 0:SEQ + 2:SEQ + 1], 0.0, raw.free)
                    for bank, done, t, width in project(w, ld, hT, [h_done]):
                        m = AC.act(raw.ap[:, 1 + t:1 + t + width], bank.ap[:], ACT.Copy, [done, *raw.free])
                        psum.give(bank, m)
                    tap = lambda k: col("conv_w", k * 2 * FT + j)
                    a = DVE.ts(dst.ap[:, 0:SEQ], raw.ap[:, 1:SEQ + 1], tap(1), col("conv_b", j), ALU.mult, ALU.add,
                               [m, *dst.free])
                    a = DVE.stt(dst.ap[:, 0:SEQ], raw.ap[:, 0:SEQ], tap(0), dst.ap[:, 0:SEQ], ALU.mult, ALU.add, [a, z])
                    a = DVE.stt(dst.ap[:, 0:SEQ], raw.ap[:, 2:SEQ + 2], tap(2), dst.ap[:, 0:SEQ], ALU.mult, ALU.add, [a])
                    tiles.give(raw, a)
                    return dst, a

                f0 = 0
                out_marks = []
                for nf in (6, 6, 5, 5):
                    done_act = []
                    for j in range(f0, f0 + nf):
                        gt, gm = convolved(j)
                        vt, vm = convolved(FT + j)
                        a = acts.take()
                        m = AC.act(a.ap, gt.ap[:, 0:SEQ], ACT.Silu, [gm, *a.free])
                        tiles.give(gt, m)
                        m = DVE.tt(a.ap, a.ap, vt.ap[:, 0:SEQ], ALU.mult, [m, vm])
                        tiles.give(vt, m)
                        done_act.append((a, m))
                    ws = out_weights(w_down[f0:f0 + nf], nf, oring)
                    for t in range(TT):
                        banks = output_product(None, ws, lambda k: done_act[k][0].ap, nf, t, [m for _, m in done_act])
                        m = residual_tile(X, t, banks, [g_done, *x_read])
                        if f0 + nf == FT:
                            m_sq = AC.act(sq[:], X[:, t, :], ACT.Square, [m, m_sq], accum_out=ss[:, t:t + 1])
                            m = rsqrt(ss[:, t:t + 1], ss[:, t:t + 1], [m_sq], 1.0 / D, eps_n)
                            m = DVE.stt(X[:, t, :], X[:, t, :], ss[:, t:t + 1], gain_row, ALU.mult, ALU.mult,
                                        [m, f_done])
                            out_marks.append(m)
                    release(ws, banks[-1][1])
                    for a, _ in done_act:
                        acts.give(a, banks[-1][1])
                    f0 += nf
                stored = sem("stored")
                for t in range(TT):
                    DMA.wait([out_marks[t]])
                    DMA.program.append(lambda e, t=t: e.dma_start(out[t * P:(t + 1) * P, :], X[:, t, :]).then_inc(stored, 16))
                DMA.program.append(lambda e: e.wait_ge(stored, 16 * TT))

        block = stack.enter_context(nc.Block())

        @block.sync
        def _(e):
            for step in DMA.program:
                step(e)

        @block.tensor
        def _(e):
            for step in PE.program:
                step(e)

        @block.vector
        def _(e):
            for step in DVE.program:
                step(e)

        @block.scalar
        def _(e):
            for step in AC.program:
                step(e)

        @block.gpsimd
        def _(e):
            for step in POOL.program:
                step(e)


def kernel(**inputs):
    import concourse.bacc as bacc
    from concourse.bass_utils import run_bass_kernel_spmd

    arrays = layouts({k: np.asarray(v) for k, v in inputs.items()})
    nc = bacc.Bacc("TRN2", target_bir_lowering=False, num_devices=1)
    args = [nc.dram_tensor(n, a.shape, mybir.dt.from_np(a.dtype), kind="ExternalInput").ap() for n, a in arrays.items()]
    out = nc.dram_tensor("out", [SEQ, D], F32, kind="ExternalOutput").ap()
    build(nc, *args, out)
    r = run_bass_kernel_spmd(nc, [arrays], core_ids=[0])
    return r.results[0]["out"].reshape(1, SEQ, D)


def layouts(a):
    columns = {
        "c": a["c"], "norm_g": a["norm_g"], "ada_b": a["ada_b"], "mu": a["tshift_mu"], "w0": a["decay_w0"],
        "a0": a["iclr_a0"], "k_k": a["k_k"], "k_a": a["k_a"], "r_k": a["r_k"], "ln_w": a["rwkv_ln_w"],
        "ln_b": a["rwkv_ln_b"], "sb_g": a["sb_norm_g"], "final_g": a["final_g"], "c_2": a["c_2"],
        "c_ctx_2": a["c_ctx_2"], "b_ada_2": a["b_ada_2"], "norm_g_2": a["norm_g_2"],
        "lb_logits": a["hg_lb_logits_2"], "gnorm": a["hg_gnorm_2"], "conv_w": a["ffn_conv_w_2"],
        "conv_b": a["ffn_conv_b_2"], "final_g_2": a["final_g_2"],
    }
    cols = np.ascontiguousarray(np.concatenate([columns[n].reshape(w, P) for n, w in COLUMNS], 0).T)

    def column_tiles(w):
        k, n = w.shape
        return np.ascontiguousarray(w.reshape(k // P, P, n // P, P).transpose(2, 1, 0, 3).reshape(n // P, P, k))

    row_tiles = lambda w: np.ascontiguousarray(w.reshape(-1, P, w.shape[-1]))
    fconst, iconst = constants()
    return {
        "x": a["x"].reshape(SEQ, D), "cols": cols, "fconst": fconst, "iconst": iconst,
        "lora_w": np.ascontiguousarray(np.concatenate([a["decay_w2"][0], a["iclr_a2"][0]], 0)),
        "ctx": a["ctx_2"].reshape(CTX, D),
        "w_ada": column_tiles(a["ada_w"][0]), "w_in": column_tiles(a["w_in"][0]), "w_out": row_tiles(a["w_out"][0]),
        "w_ada2": column_tiles(a["w_ada_2"][0]), "w_hg": column_tiles(a["hg_w_in_2"][0]),
        "w_hgo": row_tiles(a["hg_w_out_2"][0]), "w_up": column_tiles(a["ffn_w_up_2"][0]),
        "w_down": row_tiles(a["ffn_w_down_2"][0]),
    }
```

```python
import math
from contextlib import ExitStack

import numpy as np

import concourse.bass as bass
from concourse import mybir
from concourse.alu_op_type import AluOpType as ALU

F32 = mybir.dt.float32
I8 = mybir.dt.int8
F32R = mybir.dt.float32r
I32 = mybir.dt.int32
BF16 = mybir.dt.bfloat16
ACT = mybir.ActivationFunctionType

P = 128
SEQ = 1024
D = 1024
KT = D // P
TT = SEQ // P
BANK = 512
NB = SEQ // BANK
CTX = 256
HD = 64
HG_CHUNK = 32
PER_TILE = P // HG_CHUNK
SCORE_SCALE = 2.0 ** -30
DFF = 2816
FT = DFF // P
NORM_EPS = 1e-6
GN_EPS = 64e-5

IN_R, IN_K, IN_V, IN_Z, IN_G, SB_Q, SB_K, SB_V, SB_G = 0, 4, 8, 12, 13, 17, 21, 25, 29
HG_Q, HG_F, HG_I, HG_G = 0, 8, 24, 32

RATES = (1, 2, 0.85, 0.25)
PAUSE = (6, 4, 4, 8)
NSPREAD = 2
LATE = 30
FGROUPS = (3, 3, 3, 3, 3, 3, 2, 2)

COLUMNS = [
    ("c", 8), ("norm_g", 8), ("ada_b", 24), ("mu", 13), ("w0", 4), ("a0", 4), ("k_k", 4), ("k_a", 4),
    ("r_k", 4), ("ln_w", 4), ("ln_b", 4), ("sb_g", 4), ("final_g", 8), ("c_2", 8), ("c_ctx_2", 8),
    ("b_ada_2", 48), ("norm_g_2", 16), ("lb_logits", 32), ("gnorm", 1), ("conv_w", 3 * 2 * FT),
    ("conv_b", 2 * FT), ("final_g_2", 8),
]
COL_AT = {}
_n = 0
for _name, _w in COLUMNS:
    COL_AT[_name] = _n
    _n += _w
NCOLS = _n

FCONST = ["ident", "ones", "pair_ones", "at_or_after", "before", "key_before_query", "hg_fwd", "hg_bwd"]
ICONST = ["lt", "le"] + [f"low{n}" for n in (1, 2, 4, 8, 16, 32)] + \
         [f"up{n}" for n in (1, 2, 4, 8, 16, 32, 64)]


def constants():
    i, j = np.meshgrid(np.arange(P), np.arange(P), indexing="ij")
    f = {
        "ident": i == j, "ones": i >= 0, "pair_ones": i // HD == j // HD,
        "at_or_after": i >= j, "before": i < j,
        "key_before_query": i < j,
        "hg_fwd": (i // HG_CHUNK == j // HG_CHUNK) & (i <= j),
        "hg_bwd": (i // HG_CHUNK == j // HG_CHUNK) & (i >= j),
    }
    m = {"lt": i < j, "le": i <= j}
    for n in (1, 2, 4, 8, 16, 32, 64):
        low = (i // (2 * n) == j // (2 * n)) & (i % (2 * n) >= n) & (j % (2 * n) < n)
        m[f"low{n}"], m[f"up{n}"] = low, low.T
    return (np.concatenate([f[n].astype(np.float32) for n in FCONST], 1),
            np.concatenate([m[n].astype(np.int32) for n in ICONST], 1))


class Queue:

    def __init__(self, sem):
        self.sem, self.count, self.program, self.waited, self.tables = sem, 0, [], {}, None

    def wait(self, marks):
        for sem, value in marks:
            if self.waited.get(sem.name, 0) < value:
                self.waited[sem.name] = value
                self.program.append(lambda e, sem=sem, value=value: e.wait_ge(sem, value))

    def add(self, make, wait=(), mark=True):
        self.wait(wait)
        if not mark:
            self.program.append(make)
            return None
        self.count += 1
        self.program.append(lambda e: make(e).then_inc(self.sem, 1))
        return (self.sem, self.count)

    def last(self):
        return [(self.sem, self.count)] if self.count else []

    def act(self, out, in_, func, wait=(), **kw):
        if func in (ACT.Exp, ACT.Ln):
            if self.tables != "exp and ln":
                self.program.append(lambda e: e.preload_act_table_set("natural_log_exp_and_others"))
                self.tables = "exp and ln"
        elif func in (ACT.Sigmoid, ACT.Tanh, ACT.Silu):
            self.tables = "others"
        return self.add(lambda e: e.activation(out, in_, func, **kw), wait)

    def tt(self, out, a, b, op, wait=()):
        return self.add(lambda e: e.tensor_tensor(out, a, b, op), wait)

    def ts(self, out, a, s1, s2, op0, op1=None, wait=()):
        if op1 is None:
            return self.add(lambda e: e.tensor_scalar(out, a, s1, None, op0), wait)
        return self.add(lambda e: e.tensor_scalar(out, a, s1, s2, op0, op1), wait)

    def stt(self, out, a, s, b, op0, op1, wait=()):
        return self.add(lambda e: e.scalar_tensor_tensor(out=out, in0=a, scalar=s, in1=b, op0=op0, op1=op1), wait)

    def copy(self, out, in_, wait=()):
        return self.add(lambda e: e.tensor_copy(out, in_), wait)

    def fill(self, out, value, wait=()):
        return self.add(lambda e: e.memset(out, value), wait)

    def select(self, out, mask, data, wait=()):
        return self.add(lambda e: e.copy_predicated(out, mask, data), wait)

    def scan(self, out, d0, d1, op0, op1, wait=()):
        return self.add(lambda e: e.tensor_tensor_scan(out, d0, d1, 0.0, op0, op1), wait)

    def mm(self, out, lhsT, rhs, start, stop, wait=(), mark=False):
        return self.add(lambda e: e.matmul(out, lhsT, rhs, start=start, stop=stop, skip_group_check=True), wait, mark)

    def turn(self, out, in_, ident, wait=(), mark=False):
        return self.add(lambda e: e.transpose(out, in_, ident), wait, mark)


class Buffer:
    def __init__(self, ap, sem=None):
        self.ap, self.free, self.sem, self.loads = ap[:], [], sem, 0


class Rotation:

    def __init__(self, buffers, free=()):
        self.idle = list(buffers)
        for b in self.idle:
            b.free = list(free)

    def take(self):
        return self.idle.pop(0)

    def get(self):
        while not self.idle:
            yield
        return self.idle.pop(0)

    def give(self, buffer, *marks):
        buffer.free = list(marks)
        self.idle.append(buffer)


def build(nc, x, cols, fconst, iconst, lora_w, ctx, w_ada, w_in, w_out, w_ada2, w_hg, w_hgo, w_up, w_down, out):
    with ExitStack() as stack:
        def sb(name, shape, dt=F32, st=stack):
            return st.enter_context(nc.sbuf_tensor(name, shape, dt))

        def sem(name):
            return stack.enter_context(nc.semaphore(name))

        PE, DVE, AC, POOL, DMA = (Queue(sem(f"s_{n}")) for n in ("pe", "dve", "act", "pool", "sync"))
        psum = Rotation([Buffer(stack.enter_context(nc.psum_tensor(f"bank{i}", [P, BANK], F32))) for i in range(8)])

        def load(name, dst, src, wait=()):
            s = sem(name)
            DMA.wait(wait)
            DMA.program.append(lambda e: e.dma_start(dst, src).then_inc(s, 16))
            return (s, 16)

        colt = sb("colt", [P, NCOLS])
        fc = sb("fc", [P, len(FCONST) * P])
        ic = sb("ic", [P, len(ICONST) * P], I8)
        lora = sb("lora", [P, 4 * P])
        col_ld = load("ld_cols", colt[:], cols)
        fc_ld = load("ld_fc", fc[:], fconst)
        C = {n: fc[:, k * P:(k + 1) * P] for k, n in enumerate(FCONST)}
        M = {n: ic[:, k * P:(k + 1) * P] for k, n in enumerate(ICONST)}

        def col(name, k=0, n=1):
            at = COL_AT[name] + k
            return colt[:, at:at + n]

        small = sb("small", [P, 432])
        used = [0]

        def cells(n):
            used[0] += n
            assert used[0] <= 448
            return small[:, used[0] - n:used[0]]

        mix_dram = nc.dram_tensor("mix_kept", [KT, P, SEQ], F32).ap()
        x_dram = nc.dram_tensor("x_kept", [TT, P, D], F32).ap()
        mix_kept = [sem(f"mix_kept{k}") for k in range(KT)]
        x_kept = sem("x_kept_done")
        ring = Rotation([Buffer(sb(f"w{i}", [P, D]), sem(f"ld_w{i}")) for i in range(4)])

        def fetch(b, src):
            b.loads += 1
            DMA.wait(b.free)
            ap, s = b.ap, b.sem
            DMA.program.append(lambda e: e.dma_start(ap[:], src).then_inc(s, 16))
            return (b.sem, 16 * b.loads)

        def weights(src, to=None):
            b = (to or ring).take()
            return b, fetch(b, src)

        one = cells(1)
        eps_n = cells(1)
        eps_gn = cells(1)
        cst = [POOL.fill(one, 1.0), POOL.fill(eps_n, NORM_EPS), POOL.fill(eps_gn, GN_EPS)]

        def sigmoid(out, in_, wait, bias=None):
            kw = {"bias": bias} if bias is not None else {}
            return AC.act(out, in_, ACT.Sigmoid, wait, **kw)

        def rsqrt(out, in_, wait, scale, eps):
            m = AC.act(out, in_, ACT.Ln, [*wait, *cst], scale=scale, bias=eps)
            return AC.act(out, out, ACT.Exp, [m], scale=-0.5)

        def silu_cols(name, n):
            t = cells(n)
            m = sigmoid(t, col(name, 0, n), [col_ld])
            return t, DVE.tt(t, t, col(name, 0, n), ALU.mult, [m])

        c_act, c_done = silu_cols("c", KT)
        c2_act = cells(2 * KT)
        c2v = c2_act.rearrange("p (k two) -> p k two", two=2)
        c2_done = []
        for n, name in enumerate(("c_2", "c_ctx_2")):
            m = sigmoid(c2v[:, :, n], col(name, 0, KT), [col_ld])
            c2_done.append(DVE.tt(c2v[:, :, n], c2v[:, :, n], col(name, 0, KT), ALU.mult, [m]))

        def modulation(dst, src, first, count, act, act_done, bias, n, name, slots):
            bank = yield from psum.get()
            coming = []
            for j in range(count):
                while len(coming) + j < count and slots.idle:
                    coming.append(weights(src[first + j + len(coming)], slots))
                w, ld = coming.pop(0)
                for k in range(KT):
                    done = PE.mm(bank.ap[:, n * j:n * j + n], w.ap[:, k * P:(k + 1) * P], act(k), k == 0, k == KT - 1,
                                 [ld, *act_done, *bank.free] if k == 0 else (), mark=(k == KT - 1))
                slots.give(w, done)
                yield
            for i in range(n):
                m = DVE.tt(dst[:, i:n * count:n], bank.ap[:, i:n * count:n], col(bias, first, count), ALU.add,
                           [done, col_ld])
            psum.give(bank, m)
            modulated[name] = m

        modulated = {}
        mod1 = cells(24)
        mod2a = cells(32)
        mod2b = cells(32)

        def broadcast_row(dst, column, wait, free):
            marks, dfree = [], []
            for k in range(KT):
                if k % 4 == 0:
                    bank = psum.take()
                dg = diag.take()
                m = DVE.ts(dg.ap[:], C["ident"], column(k), None, ALU.mult, wait=[*wait, fc_ld, *dg.free])
                done = PE.mm(bank.ap[:, (k % 4) * P:(k % 4 + 1) * P], C["ones"], dg.ap[:], True, True,
                             [m, fc_ld, *bank.free], mark=True)
                diag.give(dg, done)
                if k % 4 == 3:
                    m = DVE.copy(dst[:, (k // 4) * BANK:(k // 4 + 1) * BANK], bank.ap[:], [done, *free])
                    psum.give(bank, m)
            return m

        def gain_cols(dst, norm, scale, wait):
            return DVE.stt(dst, scale, 1.0, norm, ALU.add, ALU.mult, wait)

        def to_channels(xt, nt, rstd, ready, dst, gain, shift, mod_ready, tmp, dst_free):
            marks = []
            for g in range(0, nt, 4):
                n = min(4, nt - g)
                xs = []
                for t in range(g, g + n):
                    b = tmp.take()
                    m = AC.act(b.ap[:, 0:D], xt(t), ACT.Copy, [*ready(t), *b.free], scale=rstd(t))
                    xs.append((b, m))
                for k in range(KT):
                    bank = psum.take()
                    for i, (b, m) in enumerate(xs):
                        done = PE.turn(bank.ap[:, i * P:(i + 1) * P], b.ap[:, k * P:(k + 1) * P], C["ident"],
                                       [m, fc_ld, *bank.free], mark=(i == n - 1))
                    m = DVE.ts(dst[:, k, g * P:(g + n) * P], bank.ap[:, 0:n * P], gain[:, k:k + 1], shift(k),
                               ALU.mult, ALU.add, [done, *mod_ready, *dst_free])
                    psum.give(bank, m)
                for b, _ in xs:
                    tmp.give(b, done)
                marks.append(m)
            return marks[-1]

        def project(src_w, src, ready, use, n=SEQ):
            w = yield from ring.get()
            ld = fetch(w, src_w)
            for t in range(0, n, BANK):
                bank = yield from psum.get()
                width = min(BANK, n - t)
                for k in range(KT):
                    done = PE.mm(bank.ap[:, 0:width], w.ap[:, k * P:(k + 1) * P], src[:, k, t:t + width],
                                 k == 0, k == KT - 1, [ld, *ready, *bank.free] if k == 0 else (), mark=(k == KT - 1))
                    if k % 2 == 1 and k < KT - 1:
                        yield
                if t + BANK >= n:
                    ring.give(w, done)
                m = use(bank.ap[:, 0:width], done, t, width)
                psum.give(bank, m)
                yield
            return m

        def head_sums(mat, src, ready):
            banks = []
            while len(psum.idle) < NB:
                yield
            for t in range(NB):
                bank = psum.take()
                done = PE.mm(bank.ap[:], mat, src[:, t * BANK:(t + 1) * BANK], True, True,
                             [*ready, fc_ld, *bank.free], mark=True)
                banks.append((bank, done, t * BANK, BANK))
            return banks

        def run(*parts):
            live = [[g, rate, 0.0] for g, rate in parts]
            rounds = 0
            while live:
                rounds += 1
                assert rounds < 100000, "parts wait for each other's buffers"
                for p in list(live):
                    p[2] += p[1]
                    while p[2] >= 1:
                        p[2] -= 1
                        try:
                            next(p[0])
                        except StopIteration:
                            live.remove(p)
                            break

        def pause(n):
            for _ in range(n):
                yield

        def drive(g):
            while True:
                try:
                    next(g)
                except StopIteration as e:
                    return e.value

        stats = cells(TT)
        NTILE = 22
        with ExitStack() as st:
            hT = sb("hT1", [P, KT, SEQ], st=st)
            tiles = Rotation([Buffer(sb(f"tile{i}", [P, SEQ + 2], st=st)) for i in range(NTILE)])
            half = Rotation([Buffer(sb(f"half{i}", [P, BANK], st=st)) for i in range(6)])
            lt_buf = [Buffer(sb(f"ltb{h}", [P, BANK], st=st)) for h in range(2)]
            mt_buf = [Buffer(sb(f"mtb{h}", [P, BANK], st=st)) for h in range(2)]
            rb_buf = [Buffer(sb(f"rbb{h}", [P, BANK], st=st)) for h in range(2)]
            rk_buf = [Buffer(sb(f"rkb{h}", [P, BANK], st=st)) for h in range(2)]
            t_buf = [Buffer(sb(f"tb{h}", [P, BANK], st=st)) for h in range(2)]
            tt_buf = [Buffer(sb(f"ttb{h}", [P, BANK], st=st)) for h in range(2)]
            u_buf = [Buffer(sb(f"ub{h}", [P, BANK], st=st)) for h in range(2)]
            xbuf = Rotation([Buffer(sb(f"xb{i}", [P, P], st=st)) for i in range(3)])
            mod_ring = Rotation([Buffer(sb(f"wm{i}", [P, D], st=st), sem(f"ld_wm{i}")) for i in range(2)])
            state = Buffer(sb("state", [P, P], st=st))
            state_sum = Buffer(sb("state_sum", [P, P], st=st))
            zeroed = [POOL.fill(b.ap[:], 0.0) for b in (*lt_buf, *mt_buf, *rb_buf, *rk_buf)]

            in_chunk = sb("in_chunk", [P, SEQ], BF16, st=st)
            m = POOL.fill(in_chunk[:], 1.0)
            start_done = POOL.fill(in_chunk[:, 0:SEQ:P], 0.0, [m])

            xt, x_ld = [], []
            for t in range(TT):
                b = tiles.take()
                xt.append(b)
                x_ld.append(load(f"ld_x{t}", b.ap[:, 0:D], x[t * P:(t + 1) * P, :]))
            ic_ld = []
            for i in range(0, len(ICONST), KT):
                b, n = tiles.take(), min(KT, len(ICONST) - i) * P
                wide = b.ap[:, 0:n].bitcast(I32)
                m = load(f"ld_ic{i}", wide, iconst[:, i * P:i * P + n])
                ic_ld.append(DVE.copy(ic[:, i * P:i * P + n], wide, [m]))
                tiles.give(b, ic_ld[-1])
            lora_ld = load("ld_lora", lora[:], lora_w)
            sq = tiles.take()
            marks = []
            m = None
            for t in range(TT):
                m = AC.act(sq.ap[:, 0:D], xt[t].ap[:, 0:D], ACT.Square, [x_ld[t]] + ([m] if m else []),
                           accum_out=stats[:, t:t + 1])
            tiles.give(sq, m)
            rstd_done = rsqrt(stats[:, 0:TT], stats[:, 0:TT], [m], 1.0 / D, eps_n)
            for _ in modulation(mod1, w_ada, 0, 16, lambda k: c_act[:, k:k + 1], [c_done], "ada_b", 1, "mod1", ring):
                pass
            gain1 = cells(KT)
            g1 = gain_cols(gain1, col("norm_g", 0, KT), mod1[:, 8:16], [modulated["mod1"], col_ld])
            h_done = to_channels(lambda t: xt[t].ap[:, 0:D], TT, lambda t: stats[:, t:t + 1],
                                 lambda t: [rstd_done], hT, gain1, lambda k: mod1[:, k:k + 1], [g1],
                                 tiles, [])
            for b in xt:
                tiles.give(b, *AC.last())

            par_done = []
            keep_mu = cells(13)
            omka = cells(4)
            par_done.append(DVE.ts(keep_mu, col("mu", 0, 13), -1.0, 1.0, ALU.mult, ALU.add, [col_ld]))
            par_done.append(DVE.ts(omka, col("k_a", 0, 4), -1.0, 1.0, ALU.mult, ALU.add))
            decay_cols = cells(16)

            def shifted(ct):
                raw = yield from tiles.get()
                dst = yield from tiles.get()
                z = DVE.fill(raw.ap[:, 0:1], 0.0, raw.free)
                m = yield from project(w_in[ct], hT, [h_done], lambda bank, done, t, width: AC.act(
                    raw.ap[:, 1 + t:1 + t + width], bank, ACT.Copy, [done, *raw.free]))
                a = DVE.ts(dst.ap[:, 0:SEQ], raw.ap[:, 1:SEQ + 1], keep_mu[:, ct:ct + 1], None, ALU.mult,
                           wait=[m, *par_done, *dst.free])
                b = DVE.stt(dst.ap[:, 0:SEQ], raw.ap[:, 0:SEQ], col("mu", ct), dst.ap[:, 0:SEQ], ALU.mult, ALU.add,
                            [a, z])
                tiles.give(raw, b)
                return dst, b

            def silu_gate(ct):
                dst = yield from tiles.get()

                def use(bank, done, t, width):
                    m = sigmoid(dst.ap[:, t:t + width], bank, [done, *dst.free])
                    return DVE.tt(dst.ap[:, t:t + width], dst.ap[:, t:t + width], bank, ALU.mult, [m])

                m = yield from project(w_in[ct], hT, [h_done], use)
                return dst, m

            def keep_mix(k, tile, ready):
                POOL.wait([ready])
                ap, s = tile.ap[:, 0:SEQ], mix_kept[k]
                POOL.program.append(lambda e: e.dma_start(mix_dram[k], ap).then_inc(s, 16))
                tiles.give(tile, (s, 16))

            def to_tokens(src, ready):
                dst = yield from tiles.get()
                for g in range(NB):
                    bank = yield from psum.get()
                    for i in range(4):
                        at = (4 * g + i) * P
                        done = PE.turn(bank.ap[:, i * P:(i + 1) * P], src[:, at:at + P], C["ident"],
                                       [*ready, *bank.free], mark=(i == 3))
                    m = AC.act(dst.ap[:, g * BANK:(g + 1) * BANK], bank.ap[:], ACT.Copy, [done, *dst.free])
                    psum.give(bank, m)
                return dst, m, done

            zt, z_done = drive(shifted(IN_Z))
            z_done = [z_done, AC.act(zt.ap[0:HD, 0:SEQ], zt.ap[0:HD, 0:SEQ], ACT.Tanh, [z_done])]

            full = lambda b: b.ap[:, 0:SEQ]
            chunks = lambda ap: ap.rearrange("p (c t) -> p c t", t=P)
            prepared = {}
            placed = [-1]

            def rwkv_inputs():
                for ht in range(4):
                    while placed[0] < ht - 1:
                        yield
                    rT, r_done = yield from shifted(IN_R + ht)
                    kT, k_done = yield from shifted(IN_K + ht)
                    vT, v_done = yield from shifted(IN_V + ht)
                    mneg = yield from tiles.get()
                    aT = yield from tiles.get()
                    for dst, lo, base in ((mneg, 0, "w0"), (aT, HD, "a0")):
                        for t in range(NB):
                            bank = yield from psum.get()
                            done = PE.mm(bank.ap[:], lora[lo:lo + HD, ht * P:(ht + 1) * P],
                                         zt.ap[lo:lo + HD, t * BANK:(t + 1) * BANK], True, True,
                                         [*z_done, lora_ld, *bank.free], mark=True)
                            a_done = sigmoid(dst.ap[:, t * BANK:(t + 1) * BANK], bank.ap[:],
                                             [done, col_ld, *dst.free], col(base, ht))
                            psum.give(bank, a_done)
                    decay_done = DVE.ts(full(mneg), full(mneg), math.exp(-0.5), None, ALU.mult, wait=[a_done])
                    yield
                    kk = yield from tiles.get()
                    m = AC.act(full(kk), full(kT), ACT.Square, [k_done, col_ld, *kk.free], scale=col("k_k", ht))
                    yield
                    sums = yield from head_sums(C["pair_ones"], full(kk), [m])
                    for bank, done, t, width in sums:
                        m = DVE.ts(kk.ap[:, t:t + width], bank.ap[:], 1e-24, None, ALU.max, wait=[done, sums[-1][1]])
                        psum.give(bank, m)
                    m = AC.act(full(kk), full(kk), ACT.Ln, [m])
                    m = AC.act(full(kk), full(kk), ACT.Exp, [m], scale=-0.5)
                    kk_done = DVE.stt(full(kk), full(kT), col("k_k", ht), full(kk), ALU.mult, ALU.mult, [m])
                    tmp = yield from tiles.get()
                    m = DVE.ts(full(tmp), full(aT), col("k_a", ht), omka[:, ht:ht + 1], ALU.mult, ALU.add,
                               [a_done, *tmp.free])
                    k_done = DVE.tt(full(kT), full(kT), full(tmp), ALU.mult, [m, kk_done])
                    a_done = DVE.tt(full(aT), full(kk), full(aT), ALU.mult, [m, kk_done])
                    m = DVE.stt(full(tmp), full(rT), col("r_k", ht), full(kT), ALU.mult, ALU.mult, [k_done, r_done])
                    yield
                    bonus = yield from tiles.get()
                    sums = yield from head_sums(C["pair_ones"], full(tmp), [m])
                    for bank, done, t, width in sums:
                        m = DVE.tt(bonus.ap[:, t:t + width], bank.ap[:], vT.ap[:, t:t + width], ALU.mult,
                                   [done, v_done, *bonus.free])
                        psum.give(bank, m)
                    bonus_done = m
                    vtok, vtok_done, vT_read = yield from to_tokens(full(vT), [v_done, fc_ld])
                    tiles.give(vT, bonus_done, vT_read)
                    yield
                    b = yield from tiles.get()
                    m = DVE.scan(full(b), in_chunk[:], full(mneg), ALU.mult, ALU.subtract, [decay_done, start_done, *b.free])
                    bc = chunks(full(b))
                    mid, end = bc[:, :, P // 2 - 1], bc[:, :, P - 1]
                    dc = decay_cols[:, (ht % 2) * TT:(ht % 2 + 1) * TT]
                    m2 = DVE.tt(dc, end, mid, ALU.subtract, [m, *decay_free[ht % 2]])
                    m2 = DVE.tt(dc[:, 0:TT - 1], dc[:, 0:TT - 1], bc[:, 1:TT, P // 2 - 1], ALU.add, [m2])
                    dc_done = AC.act(dc, dc, ACT.Exp, [m2])
                    from_mid = DVE.tt(chunks(full(tmp)), bc, bc[:, :, P // 2 - 1:P // 2].broadcast_to([P, TT, P]),
                                      ALU.subtract, [m, done])
                    up_done = AC.act(full(b), full(tmp), ACT.Exp, [from_mid, m2])
                    r_done = DVE.tt(full(rT), full(rT), full(b), ALU.mult, [up_done, m])
                    down_done = AC.act(full(b), full(tmp), ACT.Exp, [r_done], scale=-1.0)
                    k_done = DVE.tt(full(kT), full(kT), full(b), ALU.mult, [down_done])
                    b_done = DVE.tt(full(aT), full(aT), full(b), ALU.mult, [down_done, a_done])
                    m = DVE.tt(full(tmp), full(tmp), full(mneg), ALU.add, [down_done])
                    before_done = AC.act(full(tmp), full(tmp), ACT.Exp, [m])
                    a2_done = DVE.stt(full(kk), full(kk), -1.0, full(tmp), ALU.mult, ALU.mult, [before_done])
                    tiles.give(b, k_done, b_done)
                    tiles.give(tmp, a2_done)
                    tiles.give(mneg, m)
                    prepared[ht] = (kk, aT, kT, rT, a2_done, b_done, k_done, r_done, vtok, vtok_done, bonus, bonus_done,
                                    dc, dc_done)
                    yield

            def rwkv_chain():
                for ht in range(4):
                    while ht not in prepared:
                        yield
                    (A, B, K, R, a2_done, b_done, k_done, r_done, vtok, vtok_done, bonus, bonus_done,
                     dc, dc_done) = prepared[ht]
                    ktok, ktok_done, _ = yield from to_tokens(full(K), [k_done])
                    btok, btok_done, _ = yield from to_tokens(full(B), [b_done])
                    yt = yield from tiles.get()
                    placed[0] = ht
                    st_mark = DVE.fill(state.ap[:], 0.0, state.free)
                    yield
                    for hf in range(2):
                        at = lambda i: slice((4 * hf + i) * P, (4 * hf + i + 1) * P)
                        level_done = [None, None]
                        made = {}
                        for h in range(2):
                            rows = slice(h * HD, (h + 1) * HD)
                            rep = lambda mask: mask.rearrange("p (o t) -> p o t", o=1).broadcast_to([P, 4, P])
                            quad = lambda ap: ap.rearrange("p (c t) -> p c t", t=P)
                            ti = POOL.copy(quad(t_buf[h].ap[:]), rep(C["ident"]), [fc_ld, *t_buf[h].free])
                            tti = POOL.copy(quad(tt_buf[h].ap[:]), rep(C["ident"]), [*tt_buf[h].free])
                            for name, left, right, buf, mask in (
                                    ("LT", B, A, lt_buf[h], "lt"), ("L", A, B, None, "low1"),
                                    ("MT", K, A, mt_buf[h], "lt"), ("RB", B, R, rb_buf[h], "le"),
                                    ("RK", K, R, rk_buf[h], "le")):
                                bank = yield from psum.get()
                                for i in range(4):
                                    done = PE.mm(bank.ap[:, i * P:(i + 1) * P], left.ap[rows, at(i)],
                                                 right.ap[rows, at(i)], True, True,
                                                 [a2_done, b_done, k_done, r_done, *bank.free], mark=(i == 3))
                                if name == "L":
                                    t_done = DVE.select(quad(t_buf[h].ap[:]), rep(M["low1"]), quad(bank.ap[:]),
                                                        [done, ti, *ic_ld])
                                    psum.give(bank, t_done)
                                    continue
                                made[name, h] = DVE.select(quad(buf.ap[:]), rep(M[mask]), quad(bank.ap[:]),
                                                           [done, *ic_ld, *zeroed, *buf.free])
                                psum.give(bank, made[name, h])
                                if name == "LT":
                                    tt_done = DVE.select(quad(tt_buf[h].ap[:]), rep(M["up1"]), quad(buf.ap[:]),
                                                         [made[name, h], tti])
                            level_done[h] = [t_done, tt_done, made["LT", h]]
                            yield
                        for n in (2, 4, 8, 16, 32, 64):
                            for h in range(2):
                                bank = yield from psum.get()
                                for i in range(4):
                                    s = slice(i * P, (i + 1) * P)
                                    done = PE.mm(bank.ap[:, s], lt_buf[h].ap[:, s], t_buf[h].ap[:, s], True, True,
                                                 [*level_done[h], *bank.free], mark=(i == 3))
                                u_done = AC.act(u_buf[h].ap[:], bank.ap[:], ACT.Copy, [done, *u_buf[h].free])
                                psum.give(bank, u_done)
                                level_done[h] = [u_done, *level_done[h]]
                                lt_read = done
                            yield
                            for h in range(2):
                                marks = []
                                if n < 64:
                                    bank = yield from psum.get()
                                    for i in range(4):
                                        s = slice(i * P, (i + 1) * P)
                                        done = PE.mm(bank.ap[:, s], tt_buf[h].ap[:, s], u_buf[h].ap[:, s], True, True,
                                                     [*level_done[h], *bank.free], mark=(i == 3))
                                    tb, t_wait = bank, done
                                    m = DVE.select(quad(t_buf[h].ap[:]), rep(M[f"low{n}"]), quad(tb.ap[:]), [t_wait])
                                    psum.give(tb, m)
                                    marks.append(m)
                                bank = yield from psum.get()
                                for i in range(4):
                                    s = slice(i * P, (i + 1) * P)
                                    done = PE.mm(bank.ap[:, s], u_buf[h].ap[:, s], tt_buf[h].ap[:, s], True, True,
                                                 [*level_done[h], *bank.free], mark=(i == 3))
                                u_buf[h].free = [done]
                                m = DVE.select(quad(tt_buf[h].ap[:]), rep(M[f"up{n}"]), quad(bank.ap[:]), [done])
                                psum.give(bank, m)
                                level_done[h] = [*marks, m]
                            yield
                        for h in range(2):
                            lt_buf[h].free = [lt_read]
                            t_buf[h].free = [lt_read]
                        for i in range(4):
                            c = 4 * hf + i
                            s = slice(i * P, (i + 1) * P)
                            bank = yield from psum.get()
                            PE.mm(bank.ap[:, 0:P], A.ap[:, at(i)], state.ap[:], True, False, [st_mark, *bank.free])
                            for h in range(2):
                                hc = slice(h * HD, (h + 1) * HD)
                                done = PE.mm(bank.ap[:, hc], mt_buf[h].ap[:, s], vtok.ap[:, c * P + h * HD:c * P + (h + 1) * HD],
                                             False, True, [made["MT", h], vtok_done], mark=(h == 1))
                            xs = yield from xbuf.get()
                            x_done = DVE.copy(xs.ap[:], bank.ap[:, 0:P], [done, *xs.free])
                            psum.give(bank, x_done)
                            yield
                            yb = yield from psum.get()
                            sbk = yield from psum.get()
                            PE.mm(yb.ap[:, 0:P], state.ap[:], R.ap[:, at(i)], True, False, yb.free)
                            for h in range(2):
                                hc = slice(h * HD, (h + 1) * HD)
                                PE.mm(yb.ap[hc, 0:P], vtok.ap[:, c * P + h * HD:c * P + (h + 1) * HD], rk_buf[h].ap[:, s],
                                      False, False, [made["RK", h]])
                            PE.mm(sbk.ap[:, 0:P], ktok.ap[:, c * P:(c + 1) * P], vtok.ap[:, c * P:(c + 1) * P], True, False,
                                  [ktok_done, *sbk.free])
                            bank = yield from psum.get()
                            for h in range(2):
                                hc = slice(h * HD, (h + 1) * HD)
                                done = PE.mm(bank.ap[:, hc], tt_buf[h].ap[:, s], xs.ap[:, hc], True, True,
                                             [x_done, *level_done[h], *bank.free], mark=(h == 1))
                            xbuf.give(xs, done)
                            sa = yield from xbuf.get()
                            sa_done = DVE.copy(sa.ap[:], bank.ap[:, 0:P], [done, *sa.free])
                            psum.give(bank, sa_done)
                            yield
                            st_read = PE.mm(sbk.ap[:, 0:P], btok.ap[:, c * P:(c + 1) * P], sa.ap[:], False, True,
                                            [sa_done, btok_done], mark=True)
                            m = DVE.tt(state_sum.ap[:], sbk.ap[:, 0:P], state.ap[:], ALU.add, [st_read])
                            st_mark = DVE.stt(state.ap[:], state_sum.ap[:], dc[:, c:c + 1], C["pair_ones"],
                                              ALU.mult, ALU.mult, [m, dc_done])
                            psum.give(sbk, m)
                            for h in range(2):
                                hc = slice(h * HD, (h + 1) * HD)
                                done = PE.mm(yb.ap[hc, 0:P], sa.ap[:, hc], rb_buf[h].ap[:, s], False, True,
                                             [made["RB", h]], mark=(h == 1))
                            xbuf.give(sa, done)
                            y_done = AC.act(yt.ap[:, at(i)], yb.ap[:, 0:P], ACT.Copy, [done, *yt.free])
                            psum.give(yb, y_done)
                            yield
                        for h in range(2):
                            for bf in (mt_buf, rb_buf, rk_buf, tt_buf):
                                bf[h].free = [done]
                    state.free = [done]
                    decay_free[ht % 2] = [st_mark]
                    for bf in (A, B, K, R, ktok, btok, vtok):
                        tiles.give(bf, done)
                    tmp = yield from tiles.get()
                    yield
                    sums = yield from head_sums(C["pair_ones"], full(yt), [y_done])
                    for bank, done, t, width in sums:
                        m = DVE.stt(yt.ap[:, t:t + width], bank.ap[:], -1.0 / HD, yt.ap[:, t:t + width],
                                    ALU.mult, ALU.add, [done])
                        psum.give(bank, m)
                    m = AC.act(full(tmp), full(yt), ACT.Square, [m, *tmp.free])
                    yield
                    sums = yield from head_sums(C["pair_ones"], full(tmp), [m])
                    for bank, done, t, width in sums:
                        m = rsqrt(tmp.ap[:, t:t + width], bank.ap[:], [done, sums[-1][1]], 1.0 / HD, eps_gn)
                        psum.give(bank, m)
                    m = DVE.tt(full(yt), full(yt), full(tmp), ALU.mult, [m])
                    tiles.give(tmp, m)
                    m = DVE.ts(full(yt), full(yt), col("ln_w", ht), col("ln_b", ht), ALU.mult, ALU.add, [m])
                    m = DVE.tt(full(yt), full(yt), full(bonus), ALU.add, [m, bonus_done])
                    tiles.give(bonus, m)
                    gate, gate_done = yield from silu_gate(IN_G + ht)
                    m = DVE.tt(full(yt), full(yt), full(gate), ALU.mult, [m, gate_done])
                    tiles.give(gate, m)
                    keep_mix(ht, yt, m)
                    yield

            decay_free = [[], []]

            def stick():
                for ht in range(4):
                    qk = []
                    for ct, scale in ((SB_Q, HD ** -0.5), (SB_K, 1.0)):
                        dst = yield from tiles.get()
                        m = yield from project(w_in[ct + ht], hT, [h_done], lambda bank, done, t, width: AC.act(
                            dst.ap[:, t:t + width], bank, ACT.Copy, [done, *dst.free], scale=scale))
                        qk.append((dst, m))
                    (qT, q_done), (kT, k_done) = qk
                    vT = yield from tiles.get()
                    m = yield from project(w_in[SB_V + ht], hT, [h_done], lambda bank, done, t, width: AC.act(
                        vT.ap[:, t:t + width], bank, ACT.Copy, [done, *vT.free]))
                    v, v_done, vT_read = yield from to_tokens(full(vT), [m, fc_ld])
                    tiles.give(vT, vT_read)
                    ot = yield from tiles.get()
                    for qh in range(2):
                        top = 4 * qh + 3
                        while len(psum.idle) < 3:
                            yield
                        obank, acc = psum.take(), [psum.take(), psum.take()]
                        acc_read = [[], []]
                        for kb in range(top, -1, -1):
                            q0 = max(kb * P, qh * BANK)
                            o, width = q0 - qh * BANK, qh * BANK + BANK - q0
                            on_diag = kb >= 4 * qh
                            work = []
                            for h in range(2):
                                rows = slice(h * HD, (h + 1) * HD)
                                zb = yield from psum.get()
                                done = PE.mm(zb.ap[:, 0:width], kT.ap[rows, kb * P:(kb + 1) * P],
                                             qT.ap[rows, q0:q0 + width], True, True,
                                             [q_done, k_done, *zb.free], mark=True)
                                z = yield from half.get()
                                w1 = yield from half.get()
                                zs, ws = z.ap[:, 0:width], w1.ap[:, 0:width]
                                z_done = AC.act(zs, zb.ap[:, 0:width], ACT.Copy, [done, *z.free])
                                psum.give(zb, z_done)
                                m = DVE.stt(ws, zs, -1.0, zs, ALU.mult, ALU.max, [z_done, *w1.free])
                                m = AC.act(ws, ws, ACT.Exp, [m], scale=-1.0)
                                m = AC.act(ws, ws, ACT.Ln, [m, *cst], bias=one)
                                sp = DVE.stt(ws, zs, 0.0, ws, ALU.max, ALU.add, [m])
                                if on_diag:
                                    sp = DVE.tt(ws[:, 0:P], ws[:, 0:P], C["key_before_query"], ALU.mult, [sp, fc_ld])
                                work.append((rows, z, w1, zs, ws, sp))
                            yield
                            for h, (rows, z, w1, zs, ws, sp) in enumerate(work):
                                ab = acc[h].ap[:, o:o + width]
                                s_done = PE.mm(ab, C["at_or_after"], ws, kb == top, kb == 0,
                                               [sp, *acc_read[h], *acc[h].free], mark=True)
                                m = DVE.tt(zs, zs, ab, ALU.subtract, [s_done])
                                acc_read[h] = [m]
                                if kb > 0:
                                    done = PE.mm(ab, C["before"], ws, False, False, [m], mark=True)
                                    half.give(w1, done)
                                else:
                                    half.give(w1, s_done)
                                    psum.give(acc[h], m)
                                if on_diag:
                                    m = DVE.ts(zs[:, 0:P], zs[:, 0:P], 0.0, None, ALU.min, wait=[m])
                                work[h] = (rows, z, zs, AC.act(zs, zs, ACT.Exp, [m]))
                            yield
                            for h, (rows, z, zs, m) in enumerate(work):
                                if on_diag:
                                    m = DVE.tt(zs[:, 0:P], zs[:, 0:P], C["key_before_query"], ALU.mult, [m])
                                done = PE.mm(obank.ap[rows, o:o + width], v.ap[:, kb * P + h * HD:kb * P + (h + 1) * HD], zs,
                                             kb == top, kb == 0, [m, v_done, *obank.free], mark=True)
                                half.give(z, done)
                            yield
                        m = AC.act(ot.ap[:, qh * BANK:(qh + 1) * BANK], obank.ap[:], ACT.Copy, [done, *ot.free])
                        psum.give(obank, m)
                    for bf in (qT, kT, v):
                        tiles.give(bf, done)
                    tmp = yield from tiles.get()
                    m = AC.act(tmp.ap[:, 0:SEQ], ot.ap[:, 0:SEQ], ACT.Square, [m, *tmp.free])
                    yield
                    sums = yield from head_sums(C["pair_ones"], tmp.ap[:, 0:SEQ], [m])
                    for bank, done, t, width in sums:
                        m = rsqrt(tmp.ap[:, t:t + width], bank.ap[:], [done, sums[-1][1]], 1.0 / HD, eps_n)
                        psum.give(bank, m)
                    m = DVE.stt(ot.ap[:, 0:SEQ], ot.ap[:, 0:SEQ], col("sb_g", ht), tmp.ap[:, 0:SEQ], ALU.mult, ALU.mult, [m])
                    tiles.give(tmp, m)
                    gate, gate_done = yield from silu_gate(SB_G + ht)
                    rows_of = gate.ap[:, 0:SEQ].rearrange("p (q b) -> p q b", b=TT)
                    m = DVE.tt(rows_of, rows_of, ot.ap[:, 0:SEQ].rearrange("p (b q) -> p q b", b=TT), ALU.mult,
                               [m, gate_done])
                    tiles.give(ot, m)
                    keep_mix(4 + ht, gate, m)
                    yield

            def second_modulation():
                yield from modulation(mod1[:, 16:24], w_ada, 16, 8, lambda k: c_act[:, k:k + 1], [c_done], "ada_b", 1,
                                      "gate1", mod_ring)
                yield from modulation(mod2a, w_ada2, 0, 16, lambda k: c2v[:, k, :], c2_done, "b_ada_2", 2, "mod2a", mod_ring)
                yield from modulation(mod2b, w_ada2, 16, 32, lambda k: c2v[:, k, 0:1], c2_done, "b_ada_2", 1, "mod2b", mod_ring)

            run((rwkv_chain(), RATES[0]), (rwkv_inputs(), RATES[1]), (stick(), RATES[2]), (second_modulation(), RATES[3]))

        phase = lambda: [*PE.last(), *DVE.last(), *AC.last(), *POOL.last()]

        def residual_tile(xr, t, banks, ready):
            for half_i, (bank, done) in enumerate(banks):
                s = slice(half_i * BANK, (half_i + 1) * BANK)
                tmp = prod.take()
                m = DVE.tt(tmp.ap[:], bank.ap[:], gate_row[:, s], ALU.mult, [done, *ready, *tmp.free])
                psum.give(bank, m)
                m = DVE.tt(xr[:, t, s], xr[:, t, s], tmp.ap[:], ALU.add, [m])
                prod.give(tmp, m)
            return m

        def output_product(src, ws, tile_of, nk, t, ready):
            banks = []
            for hf in range(2):
                bank = psum.take()
                for k in range(nk):
                    done = PE.mm(bank.ap[:], tile_of(k)[:, t * P:(t + 1) * P],
                                 ws[k][0].ap[:, hf * BANK:(hf + 1) * BANK], k == 0, k == nk - 1,
                                 [ws[k][1], *bank.free, *ready], mark=(k == nk - 1))
                banks.append((bank, done))
            return banks

        with ExitStack() as st:
            p1 = [*phase(), *((s, 16) for s in mix_kept)]
            rows = sb("rows", [P, 2, D], st=st)
            gate_row = rows[:, 0, :]
            gain_row = rows[:, 1, :]
            X = sb("X", [P, TT, D], st=st)
            diag = Rotation([Buffer(sb(f"diag{i}", [P, P], st=st)) for i in range(2)], p1)
            prod = Rotation([Buffer(sb(f"prod{i}", [P, BANK], st=st)) for i in range(2)], p1)
            sq = sb("sq", [P, D], BF16, st=st)
            smix = ExitStack()
            mixT = sb("mixT", [P, KT, SEQ], st=smix)
            mix_ld = [load(f"ld_mix{k}", mixT[:, k, :], mix_dram[k], [*p1, (mix_kept[k], 16)]) for k in range(KT)]

            def out_slots(scope, name, marks):
                return Rotation([Buffer(sb(f"{name}{i}", [P, D], st=scope), sem(f"ld_{name}{i}")) for i in range(6)], marks)

            x2_ld = [load(f"ld_xr{t}", X[:, t, :], x[t * P:(t + 1) * P, :], p1) for t in range(TT)]

            def out_weights(src, n, oring):
                got = []
                for k in range(n):
                    r = oring if oring.idle else ring
                    w, ld = weights(src[k], r)
                    got.append((w, ld, r))
                return got

            def release(ws, mark):
                for w, _, r in ws:
                    r.give(w, mark)

            g_done = broadcast_row(gate_row, lambda k: mod1[:, 16 + k:17 + k], [modulated["gate1"]], p1)
            f_done = broadcast_row(gain_row, lambda k: col("final_g", k), [col_ld], p1)
            so = ExitStack()
            ws = out_weights(w_out, KT, out_slots(so, "ow", p1))
            ss = cells(2 * TT)
            n_done, x_final = [], []
            m_sq = None
            for t in range(TT):
                banks = output_product(mixT, ws, lambda k: mixT[:, k, :], KT, t, mix_ld)
                m = residual_tile(X, t, banks, [g_done, x2_ld[t]])
                m_sq = AC.act(sq[:], X[:, t, :], ACT.Square, [m, *p1, *([m_sq] if m_sq else [])],
                              accum_out=ss[:, t:t + 1])
                m = rsqrt(ss[:, t:t + 1], ss[:, t:t + 1], [m_sq], 1.0 / D, eps_n)
                m = DVE.stt(X[:, t, :], X[:, t, :], ss[:, t:t + 1], gain_row, ALU.mult, ALU.mult, [m, f_done])
                x_final.append(m)
                m_sq = AC.act(sq[:], X[:, t, :], ACT.Square, [m, m_sq], accum_out=ss[:, TT + t:TT + t + 1])
                n_done.append(rsqrt(ss[:, TT + t:TT + t + 1], ss[:, TT + t:TT + t + 1], [m_sq], 1.0 / D, eps_n))
            release(ws, banks[-1][1])
            for t in range(TT):
                POOL.wait([x_final[t]])
                POOL.program.append(lambda e, t=t: e.dma_start(x_dram[t], X[:, t, :]).then_inc(x_kept, 16))
            so.close()
            p1 = phase()

            lb, lbt = cells(16), cells(32)
            l0, l1 = col("lb_logits", 0, 16), col("lb_logits", 16, 16)
            e0, mx = lbt[:, 0:16], lbt[:, 16:32]
            m = DVE.tt(mx, l0, l1, ALU.max, [col_ld])
            m2 = DVE.tt(e0, l0, mx, ALU.subtract, [m])
            m = DVE.tt(mx, l1, mx, ALU.subtract, [m2])
            m = AC.act(lbt[:], lbt[:], ACT.Exp, [m])
            m = DVE.tt(mx, e0, mx, ALU.add, [m])
            m = DVE.add(lambda e: e.reciprocal(mx, mx), [m])
            lb_done = DVE.tt(lb, e0, mx, ALU.mult, [m])
            omlb = cells(16)
            lb_done = DVE.ts(omlb, lb, -1.0, 1.0, ALU.mult, ALU.add, [lb_done])

            with ExitStack() as sh:
                hT = sb("hT2", [P, KT, SEQ], st=sh)
                tiles = Rotation([Buffer(sb(f"ht{i}", [P, SEQ], st=sh)) for i in range(7)], p1)
                hcT = sb("hcT", [P, KT, CTX], st=sh)
                vc_tiles = Rotation([Buffer(sb(f"vc{i}", [P, CTX], st=sh)) for i in range(2)], p1)
                ctx_tiles = Rotation([Buffer(sb(f"cp{i}", [P, CTX], st=sh)) for i in range(8)], p1)
                m2a = mod2a.rearrange("p (k two) -> p k two", two=2)
                gain_l, gain_c = cells(KT), cells(KT)
                gl = gain_cols(gain_l, col("norm_g_2", 0, KT), m2a[:, 8:16, 0], [modulated["mod2a"]])
                gc = gain_cols(gain_c, col("norm_g_2", 0, KT), m2a[:, 8:16, 1], [])
                cs = cells(2)
                cx = []
                for t in range(CTX // P):
                    b = tiles.take()
                    ld = load(f"ld_ctx{t}", b.ap[:, 0:D], ctx[t * P:(t + 1) * P, :], b.free)
                    m_sq = AC.act(sq[:], b.ap[:, 0:D], ACT.Square, [ld, m_sq], accum_out=cs[:, t:t + 1])
                    cx.append(b)
                c_rstd = rsqrt(cs, cs, [m_sq], 1.0 / D, eps_n)
                hc_done = to_channels(lambda t: cx[t].ap[:, 0:D], CTX // P, lambda t: cs[:, t:t + 1], lambda t: [c_rstd],
                                      hcT, gain_c, lambda k: m2a[:, k, 1:2], [gc], tiles, p1)
                for b in cx:
                    tiles.give(b, *AC.last())
                h_done = to_channels(lambda t: X[:, t, :], TT, lambda t: ss[:, TT + t:TT + t + 1], lambda t: [n_done[t]],
                                     hT, gain_l, lambda k: m2a[:, k, 0:1], [gl], tiles, p1)

                for t in range(TT):
                    tiles.give(Buffer(X[:, t, :]), (x_kept, 16 * TT), *AC.last())

                chunk_start = sb("chunk_start", [P, SEQ], BF16, st=sh)
                cs_done = POOL.fill(chunk_start[:], 1.0, p1)
                cs_done = POOL.fill(chunk_start[:, 0:SEQ:HG_CHUNK], 0.0, [cs_done])
                GROUP = 4 * PER_TILE
                NCH = SEQ // HG_CHUNK
                states_mem = [rows[:].rearrange("p a (c v) -> p (a c) v", v=P), sb("states_hi", [P, GROUP, P], st=sh)[:]]
                carry_mem = [sb(f"carry{i}", [P, P], st=sh) for i in range(2)]
                score_mem = [sb(f"scores{i}", [P, SEQ], st=sh) for i in range(2)]
                decay_mem = [cells(NCH + CTX // HG_CHUNK) for _ in range(2)]

                def forget(ct, src, ready, n, d, h, pool):
                    lf = yield from pool.get()
                    k = yield from pool.get()
                    j = d * 8 + h
                    m = yield from project(w_hg[ct], src, ready, lambda bank, done, t, width: sigmoid(
                        lf.ap[:, t:t + width], bank, [done, *lf.free]), n)
                    f = DVE.ts(lf.ap[:, 0:n], lf.ap[:, 0:n], omlb[:, j:j + 1], lb[:, j:j + 1], ALU.mult, ALU.add,
                               [m, lb_done])
                    k_done = DVE.ts(k.ap[:, 0:n], lf.ap[:, 0:n], -1.0, 1.0, ALU.mult, ALU.add, [f, *k.free])
                    lf_done = AC.act(lf.ap[:, 0:n], lf.ap[:, 0:n], ACT.Ln, [k_done])
                    return lf, lf_done, k, k_done

                def running(lf, ready, dst, n, d):
                    step = 1 if d == 0 else -1
                    return DVE.scan(dst.ap[:, 0:n][:, ::step], chunk_start[:, 0:n], lf.ap[:, 0:n][:, ::step],
                                    ALU.mult, ALU.add, [ready, cs_done, *dst.free])

                by_chunk = lambda ap: ap.rearrange("p (c t) -> p c t", t=HG_CHUNK)

                def to_end(b, ready, dst, k, k_done, n, d):
                    last = HG_CHUNK - 1 if d == 0 else 0
                    bc = by_chunk(b.ap[:, 0:n])
                    m = DVE.tt(by_chunk(dst.ap[:, 0:n]), bc[:, :, last:last + 1].broadcast_to([P, n // HG_CHUNK, HG_CHUNK]),
                               bc, ALU.subtract, [ready, *dst.free])
                    m = AC.act(dst.ap[:, 0:n], dst.ap[:, 0:n], ACT.Exp, [m])
                    return DVE.tt(dst.ap[:, 0:n], dst.ap[:, 0:n], k.ap[:, 0:n], ALU.mult, [m, k_done])

                def tokens_of(src, ready, dst, n):
                    for g in range(0, n // P, 4):
                        bank = yield from psum.get()
                        w = min(4, n // P - g)
                        for i in range(w):
                            at = (g + i) * P
                            done = PE.turn(bank.ap[:, i * P:(i + 1) * P], src.ap[:, at:at + P], C["ident"],
                                           [ready, *bank.free], mark=(i == w - 1))
                        m = AC.act(dst.ap[:, g * P:(g + w) * P], bank.ap[:, 0:w * P], ACT.Copy, [done, *dst.free])
                        psum.give(bank, m)
                    return m, done

                def chunk_products(kt, kt_done, v, v_done, p):
                    sp = yield from spread.get()
                    at = slice(p * P, (p + 1) * P)
                    v_rep = v.ap[:, at].rearrange("p (o t) -> p o t", o=1).broadcast_to([P, PER_TILE, P])
                    m = POOL.tt(sp.ap.rearrange("p (c t) -> p c t", t=P), v_rep,
                                own_rows.rearrange("p (c o) -> p c o", o=1).broadcast_to([P, PER_TILE, P]),
                                ALU.mult, [v_done, fc_ld, *sp.free])
                    yield
                    bank = yield from psum.get()
                    done = PE.mm(bank.ap[:], kt.ap[:, at], sp.ap, True, True, [m, kt_done, *bank.free], mark=True)
                    spread.give(sp, done)
                    return bank, done

                own_rows = C["hg_fwd"][:, HG_CHUNK - 1:P:HG_CHUNK]
                spread = Rotation([Buffer(sb(f"spread{i}", [P, PER_TILE * P], st=sh)) for i in range(NSPREAD)], p1)

                def hgrn(part):
                    states, carry, scores, decays = states_mem[part], carry_mem[part], score_mem[part], decay_mem[part]
                    dec, cdec = decays[:, 0:NCH], decays[:, NCH:]
                    states_free, scores_free = list(p1), list(p1)
                    carry_mark = DVE.fill(carry[:], 0.0, p1)
                    n = SEQ
                    for h in range(part, 8, 2):
                        vT = yield from ctx_tiles.get()
                        vc = yield from vc_tiles.get()
                        m = yield from project(w_hg[HG_I + h], hcT, [hc_done], lambda bank, done, t, width: AC.act(
                            vT.ap[:, t:t + width], bank, ACT.Copy, [done, *vT.free]), CTX)
                        vc_done, vT_read = yield from tokens_of(vT, m, vc, CTX)
                        ctx_tiles.give(vT, vT_read)
                        vT = yield from tiles.get()
                        m = yield from project(w_hg[HG_I + h], hT, [h_done], lambda bank, done, t, width: AC.act(
                            vT.ap[:, t:t + width], bank, ACT.Copy, [done, *vT.free]))
                        v = yield from tiles.get()
                        v_done, vT_read = yield from tokens_of(vT, m, v, n)
                        tiles.give(vT, vT_read)
                        q = yield from tiles.get()

                        def use_q(bank, done, t, width):
                            m = sigmoid(q.ap[:, t:t + width], bank, [done, *q.free])
                            return DVE.tt(q.ap[:, t:t + width], q.ap[:, t:t + width], bank, ALU.mult, [m])

                        q_done = yield from project(w_hg[HG_Q + h], hT, [h_done], use_q)
                        o = yield from tiles.get()
                        for d in range(2):
                            last = HG_CHUNK - 1 if d == 0 else 0
                            lf, lf_done, k, k_done = yield from forget(HG_F + 8 * d + h, hcT, [hc_done], CTX, d, h, ctx_tiles)
                            b = yield from ctx_tiles.get()
                            m = running(lf, lf_done, b, CTX, d)
                            dec_done = AC.act(cdec, by_chunk(b.ap[:, 0:CTX])[:, :, last], ACT.Exp, [m, carry_mark])
                            kd_done = to_end(b, m, lf, k, k_done, CTX, d)
                            ctx_tiles.give(k, kd_done)
                            yield from pause(PAUSE[2])
                            kt_done, kd_read = yield from tokens_of(lf, kd_done, b, CTX)
                            ctx_tiles.give(lf, kd_read)
                            carry_mark = DVE.fill(carry[:], 0.0, [carry_mark])
                            for p in ((0, 1) if d == 0 else (1, 0)):
                                bank, done = yield from chunk_products(b, kt_done, vc, vc_done, p)
                                for c in (range(PER_TILE) if d == 0 else range(PER_TILE - 1, -1, -1)):
                                    i = PER_TILE * p + c
                                    carry_mark = DVE.stt(carry[:], carry[:], cdec[:, i:i + 1], bank.ap[:, c * P:(c + 1) * P],
                                                         ALU.mult, ALU.add, [done, carry_mark, dec_done])
                                psum.give(bank, carry_mark)
                            ctx_tiles.give(b, done)
                            if d == 1:
                                vc_tiles.give(vc, *POOL.last())
                            yield
                            lf, lf_done, k, k_done = yield from forget(HG_F + 8 * d + h, hT, [h_done], n, d, h, tiles)
                            b = yield from tiles.get()
                            b_done = running(lf, lf_done, b, n, d)
                            bc = by_chunk(b.ap)
                            dec_done = AC.act(dec, bc[:, :, last], ACT.Exp, [b_done, carry_mark])
                            kd_done = to_end(b, b_done, lf, k, k_done, n, d)
                            yield from pause(PAUSE[0])
                            kt = yield from tiles.get()
                            kt_done, kd_read = yield from tokens_of(lf, kd_done, kt, n)
                            yield
                            qe = yield from tiles.get()
                            ref = HG_CHUNK // 2 if d == 0 else HG_CHUNK // 2 - 1
                            m = DVE.tt(by_chunk(lf.ap), bc, bc[:, :, ref:ref + 1].broadcast_to([P, NCH, HG_CHUNK]),
                                       ALU.subtract, [kd_read])
                            e1 = AC.act(qe.ap, lf.ap, ACT.Exp, [m, *qe.free])
                            qe_done = DVE.stt(qe.ap, qe.ap, SCORE_SCALE, q.ap, ALU.mult, ALU.mult, [e1, q_done])
                            e2 = AC.act(lf.ap, lf.ap, ACT.Exp, [e1], scale=-1.0)
                            ke_done = DVE.tt(k.ap, k.ap, lf.ap, ALU.mult, [e2])
                            tiles.give(lf, ke_done)
                            m = AC.act(b.ap, b.ap, ACT.Exp, [m, dec_done])
                            qb_done = DVE.tt(b.ap, b.ap, q.ap, ALU.mult, [m])
                            yield from pause(PAUSE[3])
                            mask = C["hg_fwd" if d == 0 else "hg_bwd"].rearrange("p (o t) -> p o t", o=1).broadcast_to([P, 4, P])
                            quad = lambda ap: ap.rearrange("p (c t) -> p c t", t=P)
                            for g in range(2):
                                bank = yield from psum.get()
                                for i in range(4):
                                    at = slice((4 * g + i) * P, (4 * g + i + 1) * P)
                                    done = PE.mm(bank.ap[:, i * P:(i + 1) * P], k.ap[:, at], qe.ap[:, at], True, True,
                                                 [qe_done, ke_done, *bank.free], mark=(i == 3))
                                sc_done = DVE.stt(quad(scores[:, g * BANK:(g + 1) * BANK]), quad(bank.ap[:]),
                                                  1.0 / SCORE_SCALE, mask, ALU.mult, ALU.mult, [done, *scores_free])
                                psum.give(bank, sc_done)
                                yield
                            tiles.give(k, done)
                            tiles.give(qe, done)
                            for g in ((0, 1) if d == 0 else (1, 0)):
                                order = range(4) if d == 0 else range(3, -1, -1)
                                for i in order:
                                    bank, done = yield from chunk_products(kt, kt_done, v, v_done, 4 * g + i)
                                    for c in (range(PER_TILE) if d == 0 else range(PER_TILE - 1, -1, -1)):
                                        at = PER_TILE * i + c
                                        here = states[:, at, :]
                                        if at == (0 if d == 0 else GROUP - 1):
                                            carry_mark = DVE.copy(here, carry[:], [carry_mark, *states_free])
                                        nx = at + (1 if d == 0 else -1)
                                        to = states[:, nx, :] if 0 <= nx < GROUP else carry[:]
                                        carry_mark = DVE.stt(to, here, dec[:, GROUP * g + at:GROUP * g + at + 1],
                                                             bank.ap[:, c * P:(c + 1) * P], ALU.mult, ALU.add,
                                                             [done, carry_mark, dec_done])
                                    psum.give(bank, carry_mark)
                                yield from pause(PAUSE[1])
                                bank = yield from psum.get()
                                for i in range(4):
                                    p = 4 * g + i
                                    ob = bank.ap[:, i * P:(i + 1) * P]
                                    PE.mm(ob, v.ap[:, p * P:(p + 1) * P], scores[:, p * P:(p + 1) * P],
                                          i == 0, False, [sc_done, *bank.free])
                                    for c in range(PER_TILE):
                                        at = p * P + c * HG_CHUNK
                                        od = PE.mm(ob[:, c * HG_CHUNK:(c + 1) * HG_CHUNK], states[:, PER_TILE * i + c, :],
                                                   b.ap[:, at:at + HG_CHUNK], False, i == 3 and c == PER_TILE - 1,
                                                   [carry_mark, qb_done], mark=(i == 3 and c == PER_TILE - 1))
                                states_free = [od]
                                cols_of = slice(g * BANK, (g + 1) * BANK)
                                if d == 0:
                                    o_done = AC.act(o.ap[:, cols_of], bank.ap[:], ACT.Copy, [od, *o.free])
                                else:
                                    o_done = DVE.tt(o.ap[:, cols_of], o.ap[:, cols_of], bank.ap[:], ALU.add, [od, *o_first])
                                psum.give(bank, o_done)
                                yield
                            if d == 0:
                                o_first = [o_done]
                            scores_free = [od]
                            tiles.give(b, od)
                            tiles.give(kt, done)
                        tiles.give(v, od, *POOL.last())
                        tiles.give(q, qb_done)
                        tmp = yield from tiles.get()
                        m = AC.act(tmp.ap, o.ap, ACT.Square, [o_done, *tmp.free])
                        yield
                        sums = yield from head_sums(C["ones"], tmp.ap, [m])
                        for bank, done, t, width in sums:
                            m = rsqrt(tmp.ap[:, t:t + width], bank.ap[:], [done, sums[-1][1]], 1.0 / P, eps_n)
                            psum.give(bank, m)
                        o_done = DVE.stt(o.ap, o.ap, col("gnorm"), tmp.ap, ALU.mult, ALU.mult, [m])
                        tiles.give(tmp, o_done)

                        def use_gate(bank, done, t, width):
                            dst = mixT[:, h, t:t + width]
                            m = sigmoid(dst, bank, [done, *p1])
                            return DVE.tt(dst, dst, bank, ALU.mult, [m])

                        m = yield from project(w_hg[HG_G + h], hT, [h_done], use_gate)
                        m = DVE.tt(mixT[:, h, :], mixT[:, h, :], o.ap, ALU.mult, [m, o_done])
                        tiles.give(o, m)
                        hg_mix.append(m)
                        yield

                hg_mix = []

                def late(part):
                    yield from pause(LATE)
                    yield from part

                run((hgrn(0), 1), (late(hgrn(1)), 1))

            p2 = phase()
            x3_ld = [load(f"ld_xb{t}", X[:, t, :], x_dram[t], [*p2, (x_kept, 16 * TT)]) for t in range(TT)]
            g_done = broadcast_row(gate_row, lambda k: mod2b[:, k:k + 1], [modulated["mod2b"]], p2)
            ws = out_weights(w_hgo, KT, out_slots(smix, "hw", p2))
            n_done = []
            for t in range(TT):
                banks = output_product(mixT, ws, lambda k: mixT[:, k, :], KT, t, hg_mix)
                m = residual_tile(X, t, banks, [g_done, x3_ld[t], *p2])
                m_sq = AC.act(sq[:], X[:, t, :], ACT.Square, [m, m_sq], accum_out=ss[:, t:t + 1])
                n_done.append(rsqrt(ss[:, t:t + 1], ss[:, t:t + 1], [m_sq], 1.0 / D, eps_n))
            release(ws, banks[-1][1])
            smix.close()
            p2 = phase()

            with ExitStack() as sf:
                hT_high = sb("hT_high", [P, KT, SEQ], F32R, st=sf)
                hT_low = sb("hT_low", [P, KT, SEQ], F32R, st=sf)
                parts_of_w = Rotation([Buffer(sb(f"wp{i}", [P, 2, D], F32R, st=sf)) for i in range(2)], p2)
                tiles = Rotation([Buffer(sb(f"ft{i}", [P, SEQ + 2], st=sf)) for i in range(4)], p2)
                acts = Rotation([Buffer(sb(f"fa{i}", [P, SEQ], st=sf)) for i in range(FGROUPS[0] + 1)], p2)
                oring = Rotation([Buffer(sb(f"fw{i}", [P, D], st=sf), sem(f"ld_fw{i}")) for i in range(FGROUPS[0])], p2)

                def split(high, low, src, ready):
                    m = AC.act(high, src, ACT.Copy, ready)
                    return DVE.tt(low, src, high.bitcast(F32), ALU.subtract, [m])

                gain_f = cells(KT)
                gf = gain_cols(gain_f, col("norm_g_2", KT, KT), mod2b[:, 16:24], [modulated["mod2b"]])
                for g in range(0, TT, 4):
                    xs = []
                    for t in range(g, g + 4):
                        b = tiles.take()
                        m = AC.act(b.ap[:, 0:D], X[:, t, :], ACT.Copy, [n_done[t], *b.free], scale=ss[:, t:t + 1])
                        xs.append((b, m))
                    for k in range(KT):
                        bank, tmp = psum.take(), prod.take()
                        for i, (b, m) in enumerate(xs):
                            done = PE.turn(bank.ap[:, i * P:(i + 1) * P], b.ap[:, k * P:(k + 1) * P], C["ident"],
                                           [m, fc_ld, *bank.free], mark=(i == 3))
                        m = DVE.ts(tmp.ap, bank.ap[:], gain_f[:, k:k + 1], mod2b[:, 8 + k:9 + k], ALU.mult, ALU.add,
                                   [done, gf, *tmp.free])
                        psum.give(bank, m)
                        cols_of = slice(g * P, (g + 4) * P)
                        h_done = split(hT_high[:, k, cols_of], hT_low[:, k, cols_of], tmp.ap, [m, *p2])
                        prod.give(tmp, h_done)
                    for b, _ in xs:
                        tiles.give(b, done)
                x_read = AC.last()
                g_done = broadcast_row(gate_row, lambda k: mod2b[:, 24 + k:25 + k], [modulated["mod2b"]], [m, *p2])
                f_done = broadcast_row(gain_row, lambda k: col("final_g_2", k), [col_ld], p2)

                coming = []

                def prepare(j):
                    w, ld = weights(w_up[j])
                    wp = parts_of_w.take()
                    m = split(wp.ap[:, 0, :], wp.ap[:, 1, :], w.ap, [ld, *wp.free])
                    ring.give(w, m)
                    coming.append((wp, m))

                def convolved(following, j, dst):
                    if following is not None:
                        prepare(following)
                    wp, w_done = coming.pop(0)
                    raw = tiles.take()
                    z = DVE.fill(raw.ap[:, 0:SEQ + 2:SEQ + 1], 0.0, raw.free)
                    for t in range(0, SEQ, BANK):
                        bank = psum.take()
                        for k in range(KT):
                            for i, (wi, src) in enumerate(((0, hT_low), (1, hT_high), (0, hT_high))):
                                done = PE.mm(bank.ap[:], wp.ap[:, wi, k * P:(k + 1) * P], src[:, k, t:t + BANK],
                                             k == 0 and i == 0, k == KT - 1 and i == 2,
                                             [w_done, h_done, *bank.free], mark=(k == KT - 1 and i == 2))
                        m = AC.act(raw.ap[:, 1 + t:1 + t + BANK], bank.ap[:], ACT.Copy, [done, *raw.free])
                        psum.give(bank, m)
                    parts_of_w.give(wp, done)
                    tap = lambda k: col("conv_w", k * 2 * FT + j)
                    a = DVE.ts(dst.ap[:, 0:SEQ], raw.ap[:, 1:SEQ + 1], tap(1), col("conv_b", j), ALU.mult, ALU.add,
                               [m, *dst.free])
                    a = DVE.stt(dst.ap[:, 0:SEQ], raw.ap[:, 0:SEQ], tap(0), dst.ap[:, 0:SEQ], ALU.mult, ALU.add, [a, z])
                    a = DVE.stt(dst.ap[:, 0:SEQ], raw.ap[:, 2:SEQ + 2], tap(2), dst.ap[:, 0:SEQ], ALU.mult, ALU.add, [a])
                    tiles.give(raw, a)
                    return a

                def activated(j):
                    a, v = acts.take(), tiles.take()
                    gm = convolved(FT + j, j, a)
                    m = AC.act(a.ap, a.ap, ACT.Silu, [gm])
                    vm = convolved(j + 1 if j + 1 < FT else None, FT + j, v)
                    m = DVE.tt(a.ap, a.ap, v.ap[:, 0:SEQ], ALU.mult, [m, vm])
                    tiles.give(v, m)
                    return a, m

                out_marks = []

                def down(group, ws, final):
                    for t in range(TT):
                        banks = output_product(None, ws, lambda k: group[k][0].ap, len(group), t, [m for _, m in group])
                        m = residual_tile(X, t, banks, [g_done, *x_read])
                        if final:
                            sq_mark = AC.act(sq[:], X[:, t, :], ACT.Square, [m, *AC.last()], accum_out=ss[:, t:t + 1])
                            m = rsqrt(ss[:, t:t + 1], ss[:, t:t + 1], [sq_mark], 1.0 / D, eps_n)
                            m = DVE.stt(X[:, t, :], X[:, t, :], ss[:, t:t + 1], gain_row, ALU.mult, ALU.mult,
                                        [m, f_done])
                            out_marks.append(m)
                    release(ws, banks[-1][1])
                    for a, _ in group:
                        acts.give(a, banks[-1][1])

                prepare(0)
                f0, waiting = 0, None
                for nf in FGROUPS:
                    group, ws = [], []
                    for j in range(f0, f0 + nf):
                        group.append(activated(j))
                        if waiting:
                            down(*waiting, False)
                            waiting = None
                        ws += out_weights(w_down[j:j + 1], 1, oring)
                    waiting = group, ws
                    f0 += nf
                down(*waiting, True)
                stored = sem("stored")
                for t in range(TT):
                    DMA.wait([out_marks[t]])
                    DMA.program.append(lambda e, t=t: e.dma_start(out[t * P:(t + 1) * P, :], X[:, t, :]).then_inc(stored, 16))
                DMA.program.append(lambda e: e.wait_ge(stored, 16 * TT))

        block = stack.enter_context(nc.Block())

        @block.sync
        def _(e):
            for step in DMA.program:
                step(e)

        @block.tensor
        def _(e):
            for step in PE.program:
                step(e)

        @block.vector
        def _(e):
            for step in DVE.program:
                step(e)

        @block.scalar
        def _(e):
            for step in AC.program:
                step(e)

        @block.gpsimd
        def _(e):
            for step in POOL.program:
                step(e)


def kernel(**inputs):
    import concourse.bacc as bacc
    from concourse.bass_utils import run_bass_kernel_spmd

    arrays = layouts({k: np.asarray(v) for k, v in inputs.items()})
    nc = bacc.Bacc("TRN2", target_bir_lowering=False, num_devices=1)
    args = [nc.dram_tensor(n, a.shape, mybir.dt.from_np(a.dtype), kind="ExternalInput").ap() for n, a in arrays.items()]
    out = nc.dram_tensor("out", [SEQ, D], F32, kind="ExternalOutput").ap()
    build(nc, *args, out)
    r = run_bass_kernel_spmd(nc, [arrays], core_ids=[0])
    return r.results[0]["out"].reshape(1, SEQ, D)


def layouts(a):
    columns = {
        "c": a["c"], "norm_g": a["norm_g"], "ada_b": a["ada_b"], "mu": a["tshift_mu"], "w0": a["decay_w0"],
        "a0": a["iclr_a0"], "k_k": a["k_k"], "k_a": a["k_a"], "r_k": a["r_k"], "ln_w": a["rwkv_ln_w"],
        "ln_b": a["rwkv_ln_b"], "sb_g": a["sb_norm_g"], "final_g": a["final_g"], "c_2": a["c_2"],
        "c_ctx_2": a["c_ctx_2"], "b_ada_2": a["b_ada_2"], "norm_g_2": a["norm_g_2"],
        "lb_logits": a["hg_lb_logits_2"], "gnorm": a["hg_gnorm_2"], "conv_w": a["ffn_conv_w_2"],
        "conv_b": a["ffn_conv_b_2"], "final_g_2": a["final_g_2"],
    }
    cols = np.ascontiguousarray(np.concatenate([columns[n].reshape(w, P) for n, w in COLUMNS], 0).T)

    def column_tiles(w):
        k, n = w.shape
        return np.ascontiguousarray(w.reshape(k // P, P, n // P, P).transpose(2, 1, 0, 3).reshape(n // P, P, k))

    row_tiles = lambda w: np.ascontiguousarray(w.reshape(-1, P, w.shape[-1]))
    fconst, iconst = constants()
    return {
        "x": a["x"].reshape(SEQ, D), "cols": cols, "fconst": fconst, "iconst": iconst,
        "lora_w": np.ascontiguousarray(np.concatenate([a["decay_w2"][0], a["iclr_a2"][0]], 0)),
        "ctx": a["ctx_2"].reshape(CTX, D),
        "w_ada": column_tiles(a["ada_w"][0]), "w_in": column_tiles(a["w_in"][0]), "w_out": row_tiles(a["w_out"][0]),
        "w_ada2": column_tiles(a["w_ada_2"][0]), "w_hg": column_tiles(a["hg_w_in_2"][0]),
        "w_hgo": row_tiles(a["hg_w_out_2"][0]), "w_up": column_tiles(a["ffn_w_up_2"][0]),
        "w_down": row_tiles(a["ffn_w_down_2"][0]),
    }
```
